# Optimizing a Trainium2 kernel written in Bass

```python
import math
import jax, jax.numpy as jnp
from jax import lax
import numpy as np

D_MODEL = 1024
BATCH = 1
SEQ = 1024
DEPTH = 1

CHUNK = 64
N_MIXERS = 2

D_FF = 2816

N_Q_HEADS = 16
N_KV_HEADS = 4
HEAD_DIM = 64
GQA_GROUP = N_Q_HEADS // N_KV_HEADS
Q_DIM = N_Q_HEADS * HEAD_DIM
KV_DIM = N_KV_HEADS * HEAD_DIM
QKV_DIM = Q_DIM + 2 * KV_DIM
WINDOW = 128
WINDOW_CHUNKS = WINDOW // CHUNK
N_PREV_CHUNKS = WINDOW_CHUNKS - 1
KEY_SPAN = WINDOW_CHUNKS * CHUNK

EXPAND = 2
D_INNER = EXPAND * D_MODEL
SSM_HEAD_DIM = 64
SSM_HEADS = D_INNER // SSM_HEAD_DIM
SSM_GROUPS = 8
HEADS_PER_GROUP = SSM_HEADS // SSM_GROUPS
D_STATE = 128
CONV_WIDTH = 4
CONV_DIM = D_INNER + 2 * SSM_GROUPS * D_STATE
IN_PROJ_DIM = D_INNER + CONV_DIM + SSM_HEADS
DT_MIN = 0.001
DT_MAX = 0.1

NORM_EPS = 1e-6

kernel_name = "hybrid_swa_sink_mamba2_macaron"

def rmsnorm(x, w):
    xf = x.astype(jnp.float32)
    y = xf * lax.rsqrt(jnp.mean(xf * xf, axis=-1, keepdims=True) + NORM_EPS)
    return (y * w.astype(jnp.float32)).astype(x.dtype)

def swiglu(h, w_gate, w_up, w_down):
    return (jax.nn.silu(h @ w_gate) * (h @ w_up)) @ w_down

def sink_window_attention(h, w_qkv, b_qkv, sinks, w_o, b_o):
    bsz, seq, _ = h.shape
    n_chunks = seq // CHUNK
    qkv = h @ w_qkv + b_qkv
    q, k, v = jnp.split(qkv, [Q_DIM, Q_DIM + KV_DIM], axis=-1)
    q = q.reshape(bsz, n_chunks, CHUNK, N_KV_HEADS, GQA_GROUP, HEAD_DIM)
    k = k.reshape(bsz, n_chunks, CHUNK, N_KV_HEADS, HEAD_DIM)
    v = v.reshape(bsz, n_chunks, CHUNK, N_KV_HEADS, HEAD_DIM)

    def band(t):
        pad = ((0, 0), (0, 0), (0, 0), (0, 0))
        parts = [jnp.pad(t, ((0, 0), (n, 0)) + pad[:3])[:, :n_chunks]
                 for n in range(N_PREV_CHUNKS, 0, -1)]
        return jnp.concatenate(parts + [t], axis=2)

    kb, vb = band(k), band(v)
    scale = 1.0 / math.sqrt(HEAD_DIM)
    scores = jnp.einsum('bcqkgd,bcskd->bckgqs', q, kb).astype(jnp.float32) * scale
    key_block = jnp.arange(KEY_SPAN) // CHUNK
    src_chunk = jnp.arange(n_chunks)[:, None] - (N_PREV_CHUNKS - key_block)[None, :]
    valid = (src_chunk >= 0)[None, :, None, None, None, :]
    scores = jnp.where(valid, scores, -jnp.inf)
    sink = sinks.astype(jnp.float32).reshape(1, 1, N_KV_HEADS, GQA_GROUP, 1, 1)
    sink = jnp.broadcast_to(sink, scores.shape[:-1] + (1,))
    probs = jax.nn.softmax(jnp.concatenate([scores, sink], axis=-1), axis=-1)[..., :-1]
    o = jnp.einsum('bckgqs,bcskd->bcqkgd', probs.astype(v.dtype), vb)
    o = o.reshape(bsz, seq, Q_DIM)
    return o @ w_o + b_o

def causal_depthwise_conv(x, w, b):
    ch = x.shape[-1]
    y = lax.conv_general_dilated(
        x, w.astype(x.dtype)[:, None, :], window_strides=(1,),
        padding=[(CONV_WIDTH - 1, 0)], dimension_numbers=('NWC', 'WIO', 'NWC'),
        feature_group_count=ch)
    return y + b.astype(x.dtype)

def mamba2_ssd(h, w_in, conv_w, conv_b, dt_bias, a_log, d_skip, norm_w, w_out):
    bsz, seq, _ = h.shape
    n_chunks = seq // CHUNK
    zxbcdt = h @ w_in
    z, xbc, dt = jnp.split(zxbcdt, [D_INNER, D_INNER + CONV_DIM], axis=-1)
    xbc = jax.nn.silu(causal_depthwise_conv(xbc, conv_w, conv_b))
    xs, bm, cm = jnp.split(xbc, [D_INNER, D_INNER + SSM_GROUPS * D_STATE], axis=-1)
    xs = xs.reshape(bsz, n_chunks, CHUNK, SSM_GROUPS, HEADS_PER_GROUP, SSM_HEAD_DIM)
    bm = bm.reshape(bsz, n_chunks, CHUNK, SSM_GROUPS, D_STATE)
    cm = cm.reshape(bsz, n_chunks, CHUNK, SSM_GROUPS, D_STATE)
    dt = jax.nn.softplus(dt.astype(jnp.float32) + dt_bias.astype(jnp.float32))
    dt = dt.reshape(bsz, n_chunks, CHUNK, SSM_GROUPS, HEADS_PER_GROUP)
    a = -jnp.exp(a_log.astype(jnp.float32)).reshape(SSM_GROUPS, HEADS_PER_GROUP)
    a_dt = (dt * a).transpose(0, 3, 4, 1, 2)
    x_dt = xs.astype(jnp.float32) * dt[..., None]
    a_cum = jnp.cumsum(a_dt, axis=-1)

    causal = jnp.tril(jnp.ones((CHUNK, CHUNK), dtype=bool))
    seg = a_cum[..., :, None] - a_cum[..., None, :]
    lmat = jnp.exp(jnp.where(causal, seg, -jnp.inf))
    cb = jnp.einsum('bclgn,bcsgn->bcgls', cm, bm).astype(jnp.float32)
    y_diag = jnp.einsum('bcgls,bgrcls,bcsgrp->bclgrp', cb, lmat, x_dt)

    decay = jnp.exp(a_cum[..., -1:] - a_cum)
    states = jnp.einsum('bclgn,bgrcl,bclgrp->bcgrpn', bm, decay, x_dt)
    chunk_decay = jnp.exp(a_cum[..., -1])

    def step(carry, inp):
        st, dec = inp
        return dec[..., None, None] * carry + st, carry

    init = jnp.zeros((bsz, SSM_GROUPS, HEADS_PER_GROUP, SSM_HEAD_DIM, D_STATE), jnp.float32)
    _, states_in = lax.scan(step, init, (jnp.moveaxis(states, 1, 0), jnp.moveaxis(chunk_decay, -1, 0)))
    states_in = jnp.moveaxis(states_in, 0, 1)
    y_off = jnp.einsum('bclgn,bcgrpn,bgrcl->bclgrp', cm, states_in, jnp.exp(a_cum))

    y = y_diag + y_off + xs.astype(jnp.float32) * d_skip.astype(jnp.float32).reshape(SSM_GROUPS, HEADS_PER_GROUP, 1)
    y = y.reshape(bsz, seq, D_INNER)
    gated = (y * jax.nn.silu(z.astype(jnp.float32))).reshape(bsz, seq, SSM_GROUPS, D_INNER // SSM_GROUPS)
    gated = gated * lax.rsqrt(jnp.mean(gated * gated, axis=-1, keepdims=True) + NORM_EPS)
    gated = gated.reshape(bsz, seq, D_INNER) * norm_w.astype(jnp.float32)
    return gated.astype(h.dtype) @ w_out

def setup_inputs(seed: int = 0) -> dict:
    key = jax.random.key(seed)
    ks = iter(jax.random.split(key, 40))
    n_attn = (DEPTH + N_MIXERS - 1) // N_MIXERS
    n_ssm = (DEPTH + N_MIXERS - 2) // N_MIXERS
    f32 = jnp.float32

    def nrm(shape, fan_in):
        return jax.random.normal(next(ks), shape, f32) * fan_in ** -0.5

    def gain(shape):
        return 1.0 + 0.02 * jax.random.normal(next(ks), shape, f32)

    def small(shape, s=0.01):
        return s * jax.random.normal(next(ks), shape, f32)

    x = jax.random.normal(next(ks), (BATCH, SEQ, D_MODEL), f32)
    u = jax.random.uniform(next(ks), (n_ssm, SSM_HEADS), f32)
    dt0 = jnp.exp(u * (math.log(DT_MAX) - math.log(DT_MIN)) + math.log(DT_MIN))
    dt_bias = dt0 + jnp.log(-jnp.expm1(-dt0))
    a_log = jnp.log(jax.random.uniform(next(ks), (n_ssm, SSM_HEADS), f32, 1.0, 16.0))
    return {
        "x": x,
        "ffn1_norm": gain((DEPTH, D_MODEL)),
        "ffn1_w_gate": nrm((DEPTH, D_MODEL, D_FF), D_MODEL),
        "ffn1_w_up": nrm((DEPTH, D_MODEL, D_FF), D_MODEL),
        "ffn1_w_down": nrm((DEPTH, D_FF, D_MODEL), D_FF),
        "mix_norm": gain((DEPTH, D_MODEL)),
        "ffn2_norm": gain((DEPTH, D_MODEL)),
        "ffn2_w_gate": nrm((DEPTH, D_MODEL, D_FF), D_MODEL),
        "ffn2_w_up": nrm((DEPTH, D_MODEL, D_FF), D_MODEL),
        "ffn2_w_down": nrm((DEPTH, D_FF, D_MODEL), D_FF),
        "attn_w_qkv": nrm((n_attn, D_MODEL, QKV_DIM), D_MODEL),
        "attn_b_qkv": small((n_attn, QKV_DIM)),
        "attn_sinks": small((n_attn, N_Q_HEADS), 0.5),
        "attn_w_o": nrm((n_attn, Q_DIM, D_MODEL), Q_DIM),
        "attn_b_o": small((n_attn, D_MODEL)),
        "ssm_w_in": nrm((n_ssm, D_MODEL, IN_PROJ_DIM), D_MODEL),
        "ssm_conv_w": nrm((n_ssm, CONV_WIDTH, CONV_DIM), CONV_WIDTH),
        "ssm_conv_b": small((n_ssm, CONV_DIM)),
        "ssm_dt_bias": dt_bias,
        "ssm_a_log": a_log,
        "ssm_d": gain((n_ssm, SSM_HEADS)),
        "ssm_norm": gain((n_ssm, D_INNER)),
        "ssm_w_out": nrm((n_ssm, D_INNER, D_MODEL), D_INNER),
        "final_norm": gain((D_MODEL,)),
    }

def reference(x, ffn1_norm, ffn1_w_gate, ffn1_w_up, ffn1_w_down, mix_norm,
              ffn2_norm, ffn2_w_gate, ffn2_w_up, ffn2_w_down,
              attn_w_qkv, attn_b_qkv, attn_sinks, attn_w_o, attn_b_o,
              ssm_w_in, ssm_conv_w, ssm_conv_b, ssm_dt_bias, ssm_a_log, ssm_d,
              ssm_norm, ssm_w_out, final_norm):
    for i in range(DEPTH):
        x = x + 0.5 * swiglu(rmsnorm(x, ffn1_norm[i]), ffn1_w_gate[i], ffn1_w_up[i], ffn1_w_down[i])
        hm = rmsnorm(x, mix_norm[i])
        j = i // N_MIXERS
        if i % N_MIXERS == 0:
            x = x + sink_window_attention(hm, attn_w_qkv[j], attn_b_qkv[j], attn_sinks[j],
                                          attn_w_o[j], attn_b_o[j])
        else:
            x = x + mamba2_ssd(hm, ssm_w_in[j], ssm_conv_w[j], ssm_conv_b[j], ssm_dt_bias[j],
                               ssm_a_log[j], ssm_d[j], ssm_norm[j], ssm_w_out[j])
        x = x + 0.5 * swiglu(rmsnorm(x, ffn2_norm[i]), ffn2_w_gate[i], ffn2_w_up[i], ffn2_w_down[i])
    return rmsnorm(x, final_norm)


_drawn_inputs = setup_inputs


def setup_inputs(seed=0):
    import zlib

    import numpy as np

    out = dict(_drawn_inputs(seed))
    spreads = {}
    factors = {'ffn1_norm': 6.908,
     'mix_norm': 8.0,
     'ffn2_norm': 21.663,
     'attn_b_qkv': 5.3,
     'attn_sinks': 8.0,
     'attn_b_o': 46.32,
     'final_norm': 8.441}
    for name, (base, spread) in spreads.items():
        noise = np.random.default_rng([zlib.crc32(name.encode()), seed]).standard_normal(out[name].shape)
        drawn = base * np.exp(spread * noise) if base else spread * noise
        out[name] = __import__('jax').numpy.asarray(drawn.astype(out[name].dtype))
    for name, factor in factors.items():
        out[name] = (out[name] * factor).astype(out[name].dtype)
    return out
```

```python
from contextlib import ExitStack

import concourse.bass as bass
from concourse import mybir

P = 128
T, D, F = 1024, 1024, 2816
TT, KD = T // P, D // P
HALF = 512
GROUP = 2 * P
GROUPS = F // GROUP
HEADS, KV_HEADS, DH, CHUNK = 16, 4, 64, 64
KV_DIM = KV_HEADS * DH
EPS = 1e-6
RING = 4

F32, F32R = mybir.dt.float32, mybir.dt.float32r
ALU, ACT, AX = mybir.AluOpType, mybir.ActivationFunctionType, mybir.AxisListType

DOWN_UNITS = 2 * TT
QKV_UNITS = 4 + 10
O_UNITS = 32
R_FFN1 = 0
R_QKV = R_FFN1 + GROUPS * DOWN_UNITS
R_O = R_QKV + 2 * QKV_UNITS
R_FFN2 = R_O + 2 * O_UNITS
S_FFN1 = 0
S_QKV = S_FFN1 + 6 * GROUPS
S_O = S_QKV + 24
S_FFN2 = S_O + 16
U_FFN1, U_FFN2 = 0, 4 * GROUPS
N_FFN1, N_MIX, N_FFN2, N_FINAL = 0, TT, 2 * TT, 3 * TT
QKV_TILES = [("v", 0, 0), ("v", 1, 0)] + [t for i in range(2)
                                          for t in [("k", i, 0)] + [("q", i, e) for e in range(4)]]
QKV_SLOT = [1, 3, 5]
Q_SLOT = {(0, 0): 4, (0, 1): 0, (1, 0): 2, (1, 1): 4}
SPLIT_AHEAD = [[16], [17], [18], [19, 20], [21], [22], [23], []]


def o_slots(group):
    if group % 2 == 0:
        return 1, 3
    return (0, 5) if group < 4 else (4, 5)


def qkv_done(n):
    half, j = divmod(n, 12)
    return R_QKV + half * QKV_UNITS + (4 if j < 2 else 4 + j - 1)


def trunk(nc, x, ffn1_norm, ffn1_w_gate, ffn1_w_up, ffn1_w_down, mix_norm, ffn2_norm,
          ffn2_w_gate, ffn2_w_up, ffn2_w_down, w_qkv, b_qkv, sinks, w_o, b_o, final_norm, out):
    ctx = ExitStack()
    base = 16512

    place = {}
    at = base
    for name, size in (("x", 32), ("hT", 64), ("w", 48), ("stage_g", 8), ("stage_u", 8),
                       ("stage_d", 8), ("act", 16), ("tmp", 8), ("hn", 8), ("norm_w", 4), ("rest", 2)):
        place[name] = at
        at += size * 1024

    def sb(name, region, shape, dt=F32, skip=0):
        return nc.alloc_sbuf_tensor_at(name, shape, dt, offset=place[region] + skip)

    x_res = sb("x_res", "x", [P, TT, D])
    hT = sb("hT", "hT", [P, 2, KD, T], F32R)
    w = sb("w", "w", [P, 6, 2, KD * P], F32R)
    w_k = w[:, :, :, :].rearrange("p s v (k c) -> p s v k c", k=KD)
    stage_g = sb("stage_g", "stage_g", [P, KD, GROUP])
    stage_u = sb("stage_u", "stage_u", [P, KD, GROUP])
    stage_d = sb("stage_d", "stage_d", [P, 2, D])
    stage_qkv = sb("stage_qkv", "stage_g", [P, 2, KD, P])
    a_T = sb("a_T", "act", [P, 2, 2, T], F32R)
    silu_g = sb("silu_g", "tmp", [P, 2, HALF])
    a_full = sb("a_full", "tmp", [P, 2, HALF], skip=4096)
    junk = sb("junk", "tmp", [P, D])
    hn = sb("hn", "hn", [P, 2, D])
    norm_w = sb("norm_w", "norm_w", [P, D])
    q_T = {key: sb(f"q_T{key[0]}{key[1]}", "w", [P, HALF // CHUNK, 4, CHUNK], skip=slot * 8192)
           for key, slot in Q_SLOT.items()}
    k_T = sb("k_T", "stage_u", [P, 2, T])
    v_at = sb("v_at", "act", [P, 2 * TT, KV_DIM])
    probs = sb("probs", "hn", [P, 4, 4, P])
    probs_T = sb("probs_T", "tmp", [P, 2, 4 * P], skip=4096)
    b_o_row = sb("b_o_row", "tmp", [P, D], skip=4096)
    ident = sb("ident", "rest", [P, P])
    v_bias = sb("v_bias", "rest", [P, KV_DIM], skip=512)
    stat = sb("stat", "rest", [P, 6, 4], skip=1536)
    SS, VAR, RVAR, R0, CORR, RSTD = range(6)
    soft = sb("soft", "rest", [P, 5, 4, 4], skip=1536 + 96)
    TOP, NEG_MAX, SINK_ARG, SINK_EXP, SUM = range(5)
    soft_inv = sb("soft_inv", "rest", [P, 4, 4], skip=1536 + 96 + 320)
    at_rest = 1536 + 96 + 320 + 64
    assert at_rest <= 2048
    place["more"] = place["rest"] + 2048
    q_bias = sb("q_bias", "more", [P, 2, 4])
    k_bias = sb("k_bias", "more", [P, 2], skip=32)
    sink_raw = sb("sink_raw", "more", [P, 2, 2, 2], skip=64)
    neg_sink = sb("neg_sink", "more", [P, 2, 2, 4], skip=96)

    with ctx:
        def sem(name):
            return ctx.enter_context(nc.semaphore(name))

        def bank(name):
            return ctx.enter_context(nc.psum_tensor(name, [P, HALF], F32))

        banks = [bank(f"bank{n}") for n in range(8)]

        x_loaded = [sem(f"x_loaded{t}") for t in range(TT)]
        norm_w_loaded = sem("norm_w_loaded")
        bias_loaded = sem("bias_loaded")
        gate_up_loaded = sem("gate_up_loaded")
        down_loaded = sem("down_loaded")
        qkv_loaded = [sem(f"qkv_loaded{s}") for s in range(2)]
        wo_loaded = [sem(f"wo_loaded{s}") for s in range(2)]
        b_o_loaded = sem("b_o_loaded")
        stored = [sem(f"stored{s}") for s in range(2)]
        ident_ready = sem("ident_ready")
        sink_ready = sem("sink_ready")
        hi_done = sem("hi_done")
        split_done = sem("split_done")
        gate_up_done = sem("gate_up_done")
        gate_up_free = sem("gate_up_free")
        silu_done = sem("silu_done")
        a_hi_done = sem("a_hi_done")
        a_ready = sem("a_ready")
        ring_full = sem("ring_full")
        ring_free = sem("ring_free")
        square_done = sem("square_done")
        var_done = sem("var_done")
        root_done = sem("root_done")
        rstd_done = sem("rstd_done")
        weighted = sem("weighted")
        hn_done = sem("hn_done")
        turned = sem("turned")
        hT_hi_done = sem("hT_hi_done")
        hT_ready = sem("hT_ready")
        dve_step = sem("dve_step")
        b_o_added = sem("b_o_added")
        v_shifted = sem("v_shifted")
        v_zeroed = sem("v_zeroed")
        scores_done = sem("scores_done")
        max_done = sem("max_done")
        exp_done = sem("exp_done")
        probs_zeroed = sem("probs_zeroed")
        inv_done = sem("inv_done")
        probs_ready = sem("probs_ready")
        probs_turned = sem("probs_turned")
        probs_T_ready = sem("probs_T_ready")
        pv_done = sem("pv_done")
        o_hi_done = sem("o_hi_done")
        o_ready = sem("o_ready")

        wq_view = w_qkv[:, 0:HEADS * DH].rearrange("(k p) (i s e c) -> i s e p k c", p=P, i=2, s=2, e=4)
        wk_view = w_qkv[:, HEADS * DH:HEADS * DH + KV_DIM].rearrange("(k p) (i c) -> i p k c", p=P, i=2)
        wv_view = w_qkv[:, HEADS * DH + KV_DIM:].rearrange("(k p) (i c) -> i p k c", p=P, i=2)
        wo_view = w_o.rearrange("(i s e p) n -> i s e p n", i=2, s=2, e=4)

        block = ctx.enter_context(nc.Block())

        @block.sync
        def _(sp):
            def row_of(vector):
                return vector.rearrange("(o n) -> o n", o=1).broadcast_to([P, D])

            def load_norm(vector, norms_before):
                if norms_before:
                    sp.wait_ge(weighted, norms_before)
                sp.dma_start(norm_w[:, :], row_of(vector)).then_inc(norm_w_loaded, 16)

            def load_gate_up(gate, up, column):
                sp.dma_start(stage_g[:, :, :], gate[:, bass.ds(column, GROUP)].rearrange("(k p) c -> p k c", p=P)
                             ).then_inc(gate_up_loaded, 16)
                sp.dma_start(stage_u[:, :, :], up[:, bass.ds(column, GROUP)].rearrange("(k p) c -> p k c", p=P)
                             ).then_inc(gate_up_loaded, 16)

            def load_down(down, row):
                sp.dma_start(stage_d[:, :, :], down[bass.ds(row, GROUP), :].rearrange("(f p) n -> p f n", p=P)
                             ).then_inc(down_loaded, 16)

            def load_groups(gate, up, down, s0):
                with sp.Fori(0, GROUPS - 1) as i:
                    sp.wait_ge(split_done, i * 6 + (s0 + 4))
                    load_gate_up(gate, up, i * GROUP + GROUP)
                    sp.wait_ge(split_done, i * 6 + (s0 + 6))
                    load_down(down, i * GROUP + GROUP)

            def load_x(t):
                sp.dma_start(x_res[:, t, :], x[t * P:(t + 1) * P, :]).then_inc(x_loaded[t], 16)

            load_x(0)
            load_norm(ffn1_norm, 0)
            load_x(1)
            load_gate_up(ffn1_w_gate, ffn1_w_up, 0)
            for t in range(2, TT):
                load_x(t)
            load_down(ffn1_w_down, 0)
            bq = b_qkv[0:HEADS * DH].rearrange("(i s e p) -> s p i e", i=2, s=2, e=4)
            bk = b_qkv[HEADS * DH:HEADS * DH + KV_DIM].rearrange("(i p) -> p i", i=2)
            bv = b_qkv[HEADS * DH + KV_DIM:].rearrange("(o n) -> o n", o=1)
            sk = sinks.rearrange("(o i s j e) -> o e i s j", o=1, i=2, s=2, j=2)
            with nc.allow_non_contiguous_dma(reason="a few hundred words of biases and sinks"):
                for s in range(2):
                    for i in range(2):
                        sp.dma_start(q_bias[64 * s:64 * s + 64, i, :], bq[s][:, i, :]).then_inc(bias_loaded, 16)
                    sp.dma_start(sink_raw[64 * s:64 * s + 64, :, :, :],
                                 sk[:, s].broadcast_to([64, 2, 2, 2])).then_inc(bias_loaded, 16)
                sp.dma_start(k_bias[:, :], bk).then_inc(bias_loaded, 16)
            sp.dma_start(v_bias[:, :], bv.broadcast_to([P, KV_DIM])).then_inc(bias_loaded, 16)

            load_groups(ffn1_w_gate, ffn1_w_up, ffn1_w_down, S_FFN1)

            load_norm(mix_norm, N_MIX)

            def load_qkv(n):
                sp.wait_ge(split_done, S_QKV - 2 if n < 2 else S_QKV + n - 1)
                kind, i, e = QKV_TILES[n % 12]
                dst = stage_qkv[:, n % 2]
                if kind == "q":
                    for s in range(2):
                        sp.dma_start(dst[:, :, 64 * s:64 * s + 64], wq_view[i, s, e]).then_inc(qkv_loaded[n % 2], 16)
                else:
                    sp.dma_start(dst, (wk_view if kind == "k" else wv_view)[i]).then_inc(qkv_loaded[n % 2], 16)

            def load_wo(m):
                sp.wait_ge(split_done, S_QKV if m < 2 else S_O + m - 1)
                i, e = divmod(m % 8, 4)
                for s in range(2):
                    sp.dma_start(stage_d[64 * s:64 * s + 64, m % 2, :], wo_view[i, s, e]).then_inc(wo_loaded[m % 2], 16)

            for n in range(2):
                load_qkv(n)
            for m in range(2):
                load_wo(m)
            sp.wait_ge(a_ready, U_FFN2)
            sp.dma_start(b_o_row[:, :], row_of(b_o)).then_inc(b_o_loaded, 16)
            for n in range(2, 24):
                load_qkv(n)
            load_norm(ffn2_norm, N_FFN2)
            for m in range(2, 16):
                load_wo(m)
            sp.wait_ge(scores_done, 32)
            load_gate_up(ffn2_w_gate, ffn2_w_up, 0)
            sp.wait_ge(split_done, S_FFN2)
            load_down(ffn2_w_down, 0)
            load_groups(ffn2_w_gate, ffn2_w_up, ffn2_w_down, S_FFN2)
            load_norm(final_norm, N_FINAL)
            for t in range(TT):
                sp.wait_ge(hn_done, N_FINAL + t + 1)
                sp.dma_start(out[t * P:(t + 1) * P, :], hn[:, t % 2, :]).then_inc(stored[t % 2], 16)
            for s in range(2):
                sp.wait_ge(stored[s], 16 * TT // 2)

        @block.gpsimd
        def _(pool):
            pool.memset(ident[:, :], 0.0).then_inc(ident_ready, 1)
            pool.wait_ge(ident_ready, 1)
            pool.affine_select(out=ident[:, :], in_=ident[:, :], compare_op=ALU.not_equal, fill=1.0,
                               base=0, pattern=[[-1, P]], channel_multiplier=1).then_inc(ident_ready, 1)

            def weigh(m):
                t = m % TT
                pool.wait_ge(norm_w_loaded, 16 * (m // TT + 1))
                if m >= N_FINAL + 2:
                    pool.wait_ge(stored[m % 2], 16 * ((m - N_FINAL) // 2))
                elif m >= 2:
                    pool.wait_ge(turned, m - 1)
                pool.tensor_tensor(hn[:, m % 2, :], x_res[:, t, :], norm_w[:, :], ALU.mult).then_inc(weighted, 1)

            for t in range(TT):
                pool.wait_ge(x_loaded[t], 16)
                weigh(N_FFN1 + t)
            for t in range(TT):
                pool.wait_ge(ring_free, RING + R_QKV - 2 * (TT - 1 - t))
                weigh(N_MIX + t)
            pool.wait_ge(b_o_loaded, 16)
            for t in range(TT):
                pool.wait_ge(square_done, N_MIX + t + 1)
                pool.tensor_tensor(x_res[:, t, :], x_res[:, t, :], b_o_row[:, :], ALU.add).then_inc(b_o_added, 1)
            pool.wait_ge(ring_full, R_QKV)
            pool.memset(v_at[0:64, 0, :], 0.0).then_inc(v_zeroed, 1)
            for b in range(32):
                pool.wait_ge(inv_done, b + 1)
                if b in (0, 1, 8, 9):
                    pool.memset(probs[:, b % 4, 0:2, 0:CHUNK], 0.0).then_inc(probs_zeroed, 1)
                    pool.wait_ge(probs_zeroed, b + 1 if b < 8 else b - 5)
                pool.tensor_tensor(probs[:, b % 4], probs[:, b % 4],
                                   soft_inv[:, b % 4, :].rearrange("p (j o) -> p j o", o=1).broadcast_to([P, 4, P]),
                                   ALU.mult).then_inc(probs_ready, 1)
            pool.wait_ge(probs_turned, 32)
            for t in range(4):
                pool.wait_ge(ring_free, RING + R_O + O_UNITS)
                weigh(N_FFN2 + t)
            for t in range(4, TT):
                pool.wait_ge(ring_free, RING + R_FFN2 - 2 * (TT - 1 - t))
                weigh(N_FFN2 + t)
            for t in range(TT):
                pool.wait_ge(ring_free, RING + R_FFN2 + GROUPS * DOWN_UNITS - 2 * (TT - 1 - t))
                weigh(N_FINAL + t)

        @block.tensor
        def _(pe):
            def three_passes(psum, parts, first, last):
                mm = None
                for n, ((w_hi, w_lo), (m_hi, m_lo)) in enumerate(parts):
                    for v, (lhs, rhs) in enumerate(((w_hi, m_hi), (w_hi, m_lo), (w_lo, m_hi))):
                        mm = pe.matmul(psum, lhs, rhs, start=(first and n == 0 and v == 0),
                                       stop=(last and n == len(parts) - 1 and v == 2))
                return mm

            def columns(slot, half, ks):
                return [((w_k[:, slot, 0, k, :], w_k[:, slot, 1, k, :]),
                         (hT[:, 0, k, half * HALF:(half + 1) * HALF], hT[:, 1, k, half * HALF:(half + 1) * HALF]))
                        for k in ks]

            def gate_up(f, half):
                three_passes(banks[2 * half][:, :], columns(f, half, range(KD)), True, True)
                return three_passes(banks[2 * half + 1][:, :], columns(2 + f, half, range(KD)), True, True)

            def turn(m):
                if m in (N_FFN1, N_MIX):
                    pe.wait_ge(ident_ready, 2) if m == N_FFN1 else pe.wait_ge(gate_up_free, 2 + U_FFN2)
                if m == N_FFN2:
                    pe.wait_ge(o_ready, 32)
                if m >= 1:
                    pe.wait_ge(hT_ready, m)
                pe.wait_ge(hn_done, m + 1)
                for k in range(KD):
                    mm = pe.transpose(banks[2 + k // 4][:, (k % 4) * P:(k % 4 + 1) * P],
                                      hn[:, m % 2, k * P:(k + 1) * P], ident[:, :])
                mm.then_inc(turned, 1)

            def first_gate_up(u0, s0, m0, pending):
                pe.wait_ge(hT_ready, m0 + 4)
                pe.wait_ge(split_done, s0 + 2)
                pe.wait_ge(gate_up_free, u0 + 1)
                pieces = [(bank_, slot, ks) for bank_, slot in ((0, 0), (1, 2)) for ks in ((0, 4), (4, 8))]
                for n, (bank_, slot, (k0, k1)) in enumerate(pieces):
                    mm = three_passes(banks[bank_][:, :], columns(slot, 0, range(k0, k1)), k0 == 0, k1 == KD)
                    if n == 3:
                        mm.then_inc(gate_up_done, 1)
                    if n >= 4 - len(pending):
                        turn(pending[n - (4 - len(pending))])

            def gate_up_unit(u0, s0, i, f, half, next_group=0):
                n = i * 4 + (u0 + 4 * next_group + 2 * f + half)
                pe.wait_ge(split_done, i * 6 + (s0 + 6 * next_group + 2 * f + 2))
                pe.wait_ge(gate_up_free, n + 1)
                gate_up(f, half).then_inc(gate_up_done, 1)

            def down_unit(r0, u0, s0, i, t, dh):
                d = 2 * t + dh
                if d == 0:
                    pe.wait_ge(split_done, i * 6 + (s0 + 6))
                if dh == 0 and t % 4 == 0:
                    pe.wait_ge(a_ready, i * 4 + (u0 + 3 + t // 4))
                pe.wait_ge(ring_free, i * DOWN_UNITS + (r0 + d + 1))
                three_passes(banks[4 + (r0 + d) % RING][:, :],
                             [((a_T[:, 0, f, t * P:(t + 1) * P], a_T[:, 1, f, t * P:(t + 1) * P]),
                               (w[:, 4 + f, 0, dh * HALF:(dh + 1) * HALF], w[:, 4 + f, 1, dh * HALF:(dh + 1) * HALF]))
                              for f in range(2)], True, True).then_inc(ring_full, 1)

            def swiglu(r0, u0, s0, m_next):
                with pe.Fori(0, GROUPS - 1) as i:
                    gate_up_unit(u0, s0, i, 0, 1)
                    gate_up_unit(u0, s0, i, 1, 0)
                    gate_up_unit(u0, s0, i, 1, 1)
                    for t in range(TT):
                        for dh in range(2):
                            down_unit(r0, u0, s0, i, t, dh)
                    gate_up_unit(u0, s0, i, 0, 0, next_group=1)
                i = GROUPS - 1
                gate_up_unit(u0, s0, i, 0, 1)
                gate_up_unit(u0, s0, i, 1, 0)
                gate_up_unit(u0, s0, i, 1, 1)
                for t in range(TT):
                    for dh in range(2):
                        down_unit(r0, u0, s0, i, t, dh)
                    if m_next is not None and t >= 2:
                        turn(m_next + t - 2)

            for t in range(4):
                turn(N_FFN1 + t)
            first_gate_up(U_FFN1, S_FFN1, N_FFN1, [N_FFN1 + t for t in range(4, TT)])
            pe.wait_ge(hT_ready, N_FFN1 + TT)
            swiglu(R_FFN1, U_FFN1, S_FFN1, N_MIX)

            def v_unit(half, j):
                r = R_QKV + half * QKV_UNITS + j
                if j == 0:
                    pe.wait_ge(hT_ready, N_MIX + 4 * half + 4)
                    pe.wait_ge(split_done, S_QKV + 12 * half + 2)
                pe.wait_ge(ring_free, r + 1)
                t = 4 * half + j
                slots = slice(QKV_SLOT[0], QKV_SLOT[1] + 1, QKV_SLOT[1] - QKV_SLOT[0])
                three_passes(banks[4 + r % RING][:, 0:KV_DIM],
                             [((hT[:, 0, k, t * P:(t + 1) * P], hT[:, 1, k, t * P:(t + 1) * P]),
                               (w_k[:, slots, 0, k, :], w_k[:, slots, 1, k, :]))
                              for k in range(KD)], True, True).then_inc(ring_full, 1)

            def qk_unit(half, j, part=None):
                r = R_QKV + half * QKV_UNITS + j + 2
                if part != 1:
                    pe.wait_ge(split_done, S_QKV + 12 * half + j + 1)
                    pe.wait_ge(ring_free, r + 1)
                ks = range(KD) if part is None else range(4 * part, 4 * part + 4)
                mm = three_passes(banks[4 + r % RING][:, :], columns(QKV_SLOT[j % 3], half, ks),
                                  part != 1, part != 0)
                if part != 0:
                    mm.then_inc(ring_full, 1)

            def o_unit(half, n):
                g, rest = divmod(n, 8)
                j, dh = divmod(rest, 2)
                t = 4 * half + j
                r = R_O + half * O_UNITS + n
                if rest == 0:
                    pe.wait_ge(split_done, S_O + 2 * (4 * half + g) + 2)
                pe.wait_ge(o_ready, 16 * half + 8 * (g // 2) + 2 * j + 2)
                pe.wait_ge(ring_free, r + 1)
                three_passes(banks[4 + r % RING][:, :],
                             [((hT[:, 0, 2 * g + f, t * P:(t + 1) * P], hT[:, 1, 2 * g + f, t * P:(t + 1) * P]),
                               (w[:, o_slots(4 * half + g)[f], 0, dh * HALF:(dh + 1) * HALF],
                                w[:, o_slots(4 * half + g)[f], 1, dh * HALF:(dh + 1) * HALF]))
                              for f in range(2)], True, True).then_inc(ring_full, 1)

            def scores(u):
                half, i, j = u // 8, u % 8 // 4, u % 4
                pe.wait_ge(ring_free, RING + R_QKV + half * QKV_UNITS + (9 if i == 0 else 14))
                if u >= 1:
                    pe.wait_ge(exp_done, 2 * u)
                for s in range(2):
                    rows = slice(64 * s, 64 * s + 64)
                    for cc in range(2):
                        c = 2 * (4 * half + j) + cc
                        for pair in range(2):
                            lhs = q_T[half, i][rows, 2 * j + cc, 2 * pair:2 * pair + 2, :].rearrange("p e q -> p (e q)")
                            col = (2 * cc + pair) * P
                            if c == 0:
                                for n in range(2):
                                    mm = pe.matmul(banks[s][:, col + 64 * n:col + 64 * n + 64], lhs,
                                                   k_T[rows, i, 0:64], start=True, stop=True)
                            else:
                                mm = pe.matmul(banks[s][:, col:col + P], lhs,
                                               k_T[rows, i, 64 * (c - 1):64 * (c + 1)], start=True, stop=True)
                    mm.then_inc(scores_done, 1)

            def turn_probs(u):
                for s in range(2):
                    b = 2 * u + s
                    pe.wait_ge(probs_ready, b + 1)
                    if b >= 2:
                        pe.wait_ge(o_ready, b - 1)
                    else:
                        pe.wait_ge(hT_ready, N_MIX + TT)
                    for block_ in range(4):
                        mm = pe.transpose(banks[2 + s][:, block_ * P:(block_ + 1) * P], probs[:, b % 4, block_, :], ident[:, :])
                    mm.then_inc(probs_turned, 1)

            def times_v(u):
                half, i, j = u // 8, u % 8 // 4, u % 4
                for s in range(2):
                    b = 2 * u + s
                    pe.wait_ge(probs_T_ready, b + 1)
                    if s == 0:
                        pe.wait_ge(v_shifted, 2 * (4 * half + j) + 1)
                        if u == 0:
                            pe.wait_ge(v_zeroed, 1)
                    for cc in range(2):
                        c = 2 * (4 * half + j) + cc
                        mm = pe.matmul(banks[2 + s][:, cc * 256:(cc + 1) * 256], v_at[:, c, i * P:(i + 1) * P],
                                       probs_T[:, s, cc * 256:(cc + 1) * 256], start=True, stop=True)
                    mm.then_inc(pv_done, 1)

            for j in range(4):
                v_unit(0, j)
                if j in (1, 3):
                    turn(N_MIX + 6 + j // 2)
            for j in range(2, 12):
                qk_unit(0, j)
            pe.wait_ge(hT_ready, N_MIX + TT)
            for j in range(4):
                v_unit(1, j)
            tile = 2
            for u in range(8):
                scores(u)
                if u % 4 == 0:
                    qk_unit(1, tile)
                    tile += 1
                qk_unit(1, tile, part=0)
                if u >= 1:
                    turn_probs(u - 1)
                qk_unit(1, tile, part=1)
                tile += 1
                if u >= 1:
                    times_v(u - 1)
            for u in range(8, 16):
                scores(u)
                o_unit(0, 4 * (u - 8)) if u > 8 else None
                o_unit(0, 4 * (u - 8) + 1) if u > 8 else None
                turn_probs(u - 1)
                if u == 8:
                    o_unit(0, 0)
                    o_unit(0, 1)
                o_unit(0, 4 * (u - 8) + 2)
                o_unit(0, 4 * (u - 8) + 3)
                times_v(u - 1)
            turn_probs(15)
            for n in range(4):
                o_unit(1, n)
            times_v(15)
            for n in range(4, 32):
                o_unit(1, n)
                if n in (11, 15, 19, 23):
                    turn(N_FFN2 + (n - 11) // 4)
                if n in (29, 31):
                    turn(N_FFN2 + 4 + (n - 29) // 2)

            first_gate_up(U_FFN2, S_FFN2, N_FFN2, [N_FFN2 + 6, N_FFN2 + 7])
            pe.wait_ge(hT_ready, N_FFN2 + TT)
            swiglu(R_FFN2, U_FFN2, S_FFN2, None)

        @block.scalar
        def _(act):
            def hi_of(stage, slot_view):
                act.activation(slot_view, stage, ACT.Copy).then_inc(hi_done, 1)

            def hi_gate_up(f):
                hi_of(stage_g[:, :, f * P:(f + 1) * P], w_k[:, f, 0])
                hi_of(stage_u[:, :, f * P:(f + 1) * P], w_k[:, 2 + f, 0])

            def hi_down():
                for f in range(2):
                    hi_of(stage_d[:, f, :], w[:, 4 + f, 0, :])

            def norm_front(m):
                if m >= 4:
                    act.wait_ge(rstd_done, m - 3)
                act.activation(junk[:, :], x_res[:, m % TT, :], ACT.Square,
                               accum_out=stat[:, SS, m % 4:m % 4 + 1]).then_inc(square_done, 1)
                act.wait_ge(var_done, m + 1)
                act.activation(stat[:, R0, m % 4:m % 4 + 1], stat[:, RVAR, m % 4:m % 4 + 1],
                               ACT.Sqrt).then_inc(root_done, 1)
                act.wait_ge(rstd_done, m + 1)
                act.wait_ge(weighted, m + 1)
                act.activation(hn[:, m % 2, :], hn[:, m % 2, :], ACT.Copy,
                               scale=stat[:, RSTD, m % 4:m % 4 + 1]).then_inc(hn_done, 1)

            def norm_back(m):
                t = m % TT
                act.wait_ge(turned, m + 1)
                for q in range(2):
                    act.activation(hT[:, 0, 4 * q:4 * q + 4, t * P:(t + 1) * P],
                                   banks[2 + q][:, :].rearrange("p (k c) -> p k c", k=4), ACT.Copy
                                   ).then_inc(hT_hi_done, 1)

            def hidden(u0, i, f, half):
                n = i * 4 + (u0 + 2 * f + half)
                act.wait_ge(gate_up_done, n + 1)
                act.wait_ge(gate_up_free, n + 1)
                act.activation(silu_g[:, half, :], banks[2 * half][:, :], ACT.Silu).then_inc(silu_done, 1)
                act.wait_ge(gate_up_free, n + 3)
                act.activation(a_T[:, 0, f, half * HALF:(half + 1) * HALF], a_full[:, half, :], ACT.Copy
                               ).then_inc(a_hi_done, 1)

            def swiglu(r0, u0, l0):
                with act.Fori(0, GROUPS - 1) as i:
                    hidden(u0, i, 0, 0)
                    hidden(u0, i, 0, 1)
                    act.wait_ge(gate_up_loaded, i * 32 + 32 * (l0 + 2))
                    hi_gate_up(0)
                    hidden(u0, i, 1, 0)
                    hidden(u0, i, 1, 1)
                    hi_gate_up(1)
                    act.wait_ge(down_loaded, i * 16 + 16 * (l0 + 2))
                    act.wait_ge(ring_full, i * DOWN_UNITS + (r0 + DOWN_UNITS))
                    hi_down()
                for f in range(2):
                    for half in range(2):
                        hidden(u0, GROUPS - 1, f, half)

            for t in range(TT):
                act.wait_ge(x_loaded[t], 16)
                norm_front(N_FFN1 + t)
                if t >= 1:
                    norm_back(N_FFN1 + t - 1)
                if t == 2:
                    act.wait_ge(gate_up_loaded, 32)
                    hi_gate_up(0)
                if t == 6:
                    hi_gate_up(1)
            norm_back(N_FFN1 + TT - 1)
            act.wait_ge(down_loaded, 16)
            hi_down()
            swiglu(R_FFN1, U_FFN1, 0)

            loads = [0, 0]

            def hi_qkv(n):
                loads[n % 2] += 32 if QKV_TILES[n % 12][0] == "q" else 16
                act.wait_ge(qkv_loaded[n % 2], loads[n % 2])
                if n < 3:
                    act.wait_ge(ring_full, R_QKV) if n == 2 else act.wait_ge(gate_up_done, U_FFN2)
                else:
                    act.wait_ge(ring_full, qkv_done(n - 3))
                hi_of(stage_qkv[:, n % 2], w_k[:, QKV_SLOT[n % 3], 0])

            for n in range(2):
                hi_qkv(n)
            for t in range(TT):
                act.wait_ge(ring_free, RING + R_QKV - 2 * (TT - 1 - t))
                norm_front(N_MIX + t)
                if t >= 2:
                    norm_back(N_MIX + t - 2)
            hi_qkv(2)
            norm_back(N_MIX + 6)
            norm_back(N_MIX + 7)

            def shift_v(half):
                for t in range(4 * half, 4 * half + 4):
                    act.wait_ge(ring_free, RING + R_QKV + half * QKV_UNITS + t % 4 + 1)
                    act.activation(v_at[64:128, 2 * t, :], v_at[0:64, 2 * t + 1, :], ACT.Copy).then_inc(v_shifted, 1)
                    if t < TT - 1:
                        act.activation(v_at[0:64, 2 * t + 2, :], v_at[64:128, 2 * t + 1, :], ACT.Copy
                                       ).then_inc(v_shifted, 1)

            hi_qkv(3)
            shift_v(0)
            for n in range(4, 15):
                hi_qkv(n)

            def exps(u):
                half, i, j = u // 8, u % 8 // 4, u % 4
                for s in range(2):
                    b = 2 * u + s
                    act.wait_ge(max_done, b + 1)
                    if b >= 4:
                        act.wait_ge(probs_turned, b - 3)
                    else:
                        act.wait_ge(turned, N_MIX + TT)
                    first = [n for n in range(4) if u % 4 == 0 and u < 8 and n < 2]
                    for n in range(4):
                        lo = 64 if n in first else 0
                        act.activation(probs[:, b % 4, n, lo:], banks[s][:, n * P + lo:(n + 1) * P], ACT.Exp,
                                       bias=soft[:, NEG_MAX, b % 4, n:n + 1],
                                       accum_out=soft[:, SUM, b % 4, n:n + 1])
                    act.activation(soft[:, SINK_EXP, b % 4, :], soft[:, SINK_ARG, b % 4, :], ACT.Exp
                                   ).then_inc(exp_done, 1)

            def take_probs(u):
                for s in range(2):
                    b = 2 * u + s
                    act.wait_ge(probs_turned, b + 1)
                    if b >= 2:
                        act.wait_ge(pv_done, b - 1)
                    else:
                        act.wait_ge(b_o_added, TT)
                    act.activation(probs_T[:, s, :], banks[2 + s][:, :], ACT.Copy).then_inc(probs_T_ready, 1)

            def take_outputs(u):
                half, i, j = u // 8, u % 8 // 4, u % 4
                t = 4 * half + j
                for s in range(2):
                    b = 2 * u + s
                    rows = slice(64 * s, 64 * s + 64)
                    act.wait_ge(pv_done, b + 1)
                    act.activation(
                        hT[rows, 0, 4 * i:4 * i + 4, t * P:(t + 1) * P].rearrange("p e (c q) -> p e c q", c=2),
                        banks[2 + s][rows, :].rearrange("p (c e q) -> p e c q", c=2, e=4), ACT.Copy
                    ).then_inc(o_hi_done, 1)

            def hi_wo(m):
                g = m // 2
                act.wait_ge(wo_loaded[m % 2], 32 * (m // 2 + 1))
                slot = o_slots(g)[m % 2]
                if g == 0:
                    act.wait_ge(ring_full, qkv_done(21 + m))
                elif g == 1:
                    act.wait_ge(scores_done, 16) if slot == 0 else act.wait_ge(ring_full, qkv_done(23))
                elif slot == 4 and g == 5:
                    act.wait_ge(scores_done, 32)
                else:
                    act.wait_ge(ring_full, R_O + 8 * (g - 1))
                hi_of(stage_d[:, m % 2, :], w[:, slot, 0, :])

            hi_qkv(15)
            for u in range(8):
                if u >= 2:
                    take_outputs(u - 2)
                exps(u)
                if u >= 1:
                    take_probs(u - 1)
                for n in SPLIT_AHEAD[u]:
                    hi_qkv(n)
                if u == 0:
                    shift_v(1)
            hi_wo(0)
            hi_wo(1)
            for u in range(8, 16):
                take_outputs(u - 2)
                exps(u)
                take_probs(u - 1)
                hi_wo(u - 6)
            take_outputs(14)
            take_probs(15)
            take_outputs(15)
            hi_wo(10)
            hi_wo(11)
            for t in range(4):
                act.wait_ge(ring_free, RING + R_O + O_UNITS)
                norm_front(N_FFN2 + t)
                if t >= 1:
                    norm_back(N_FFN2 + t - 1)
                hi_wo(12 + t)
            norm_back(N_FFN2 + 3)
            act.wait_ge(gate_up_loaded, 32 * (GROUPS + 1))
            hi_gate_up(0)
            for t in range(4, TT):
                act.wait_ge(ring_free, RING + R_FFN2 - 2 * (TT - 1 - t))
                norm_front(N_FFN2 + t)
                if t == 4:
                    act.wait_ge(ring_full, R_O + 8 * 7)
                    hi_gate_up(1)
                if t >= 6:
                    norm_back(N_FFN2 + t - 2)
            norm_back(N_FFN2 + 6)
            norm_back(N_FFN2 + 7)
            act.wait_ge(down_loaded, 16 * (GROUPS + 1))
            act.wait_ge(ring_full, R_FFN2)
            hi_down()
            swiglu(R_FFN2, U_FFN2, GROUPS)

            for t in range(TT):
                act.wait_ge(ring_free, RING + R_FFN2 + GROUPS * DOWN_UNITS - 2 * (TT - 1 - t))
                norm_front(N_FINAL + t)

        @block.vector
        def _(dve):
            steps = [0]

            def step(ins):
                steps[0] += 1
                ins.then_inc(dve_step, 1)
                dve.wait_ge(dve_step, steps[0])

            def lo_of(n, stage, hi, lo):
                dve.wait_ge(hi_done, n + 1)
                dve.tensor_tensor(lo, stage, hi.bitcast(F32), ALU.subtract).then_inc(split_done, 1)

            def lo_gate_up(n, f):
                lo_of(n, stage_g[:, :, f * P:(f + 1) * P], w_k[:, f, 0], w_k[:, f, 1])
                lo_of(n + 1, stage_u[:, :, f * P:(f + 1) * P], w_k[:, 2 + f, 0], w_k[:, 2 + f, 1])

            def lo_down(n):
                for f in range(2):
                    lo_of(n + f, stage_d[:, f, :], w[:, 4 + f, 0, :], w[:, 4 + f, 1, :])

            def variance(m):
                c = slice(m % 4, m % 4 + 1)
                dve.wait_ge(square_done, m + 1)
                step(dve.tensor_scalar(stat[:, VAR, c], stat[:, SS, c], 1.0 / D, EPS, ALU.mult, ALU.add))
                dve.reciprocal(stat[:, RVAR, c], stat[:, VAR, c]).then_inc(var_done, 1)

            def rstd(m):
                c = slice(m % 4, m % 4 + 1)
                dve.wait_ge(root_done, m + 1)
                step(dve.scalar_tensor_tensor(out=stat[:, CORR, c], in0=stat[:, R0, c], scalar=stat[:, R0, c],
                                              in1=stat[:, VAR, c], op0=ALU.mult, op1=ALU.mult))
                step(dve.tensor_scalar(stat[:, CORR, c], stat[:, CORR, c], -0.5, 1.5, ALU.mult, ALU.add))
                dve.tensor_tensor(stat[:, RSTD, c], stat[:, R0, c], stat[:, CORR, c], ALU.mult).then_inc(rstd_done, 1)

            def norm_front(m):
                variance(m)
                rstd(m)

            def norm_back(m):
                t = m % TT
                for q in range(2):
                    dve.wait_ge(hT_hi_done, 2 * m + q + 1)
                    ins = dve.tensor_tensor(hT[:, 1, 4 * q:4 * q + 4, t * P:(t + 1) * P],
                                            banks[2 + q][:, :].rearrange("p (k c) -> p k c", k=4),
                                            hT[:, 0, 4 * q:4 * q + 4, t * P:(t + 1) * P].bitcast(F32), ALU.subtract)
                ins.then_inc(hT_ready, 1)

            def hidden(u0, i, f, half):
                n = i * 4 + (u0 + 2 * f + half)
                dve.wait_ge(silu_done, n + 1)
                dve.tensor_tensor(a_full[:, half, :], silu_g[:, half, :], banks[2 * half + 1][:, :], ALU.mult
                                  ).then_inc(gate_up_free, 1)
                dve.wait_ge(a_hi_done, n + 1)
                cols = slice(half * HALF, (half + 1) * HALF)
                dve.tensor_tensor(a_T[:, 1, f, cols], a_full[:, half, :], a_T[:, 0, f, cols].bitcast(F32),
                                  ALU.subtract).then_inc(a_ready, 1)

            def add_to_x(r, bank_, t, dh, factor):
                dve.wait_ge(ring_full, r + 1)
                cols = x_res[:, t, dh * HALF:(dh + 1) * HALF]
                dve.scalar_tensor_tensor(out=cols, in0=banks[4 + bank_][:, :], scalar=factor, in1=cols,
                                         op0=ALU.mult, op1=ALU.add).then_inc(ring_free, 1)

            def add_down(r0, i, t):
                for dh in range(2):
                    add_to_x(i * DOWN_UNITS + (r0 + 2 * t + dh), (r0 + 2 * t + dh) % RING, t, dh, 0.5)

            def swiglu(r0, u0, s0):
                with dve.Fori(0, GROUPS - 1) as i:
                    hidden(u0, i, 0, 0)
                    hidden(u0, i, 0, 1)
                    lo_gate_up(i * 6 + (s0 + 6), 0)
                    hidden(u0, i, 1, 0)
                    hidden(u0, i, 1, 1)
                    add_down(r0, i, 0)
                    add_down(r0, i, 1)
                    lo_gate_up(i * 6 + (s0 + 8), 1)
                    for t in range(2, TT):
                        add_down(r0, i, t)
                    lo_down(i * 6 + (s0 + 10))
                for f in range(2):
                    for half in range(2):
                        hidden(u0, GROUPS - 1, f, half)

            dve.memset(stat[:, RSTD, 0:1], 0.0).then_inc(ring_free, RING)
            dve.memset(stat[:, RSTD, 1:2], 0.0).then_inc(gate_up_free, 2)

            for t in range(TT):
                norm_front(N_FFN1 + t)
                if t >= 1:
                    norm_back(N_FFN1 + t - 1)
                if t == 2:
                    lo_gate_up(S_FFN1, 0)
                if t == 6:
                    lo_gate_up(S_FFN1 + 2, 1)
            norm_back(N_FFN1 + TT - 1)
            lo_down(S_FFN1 + 4)
            dve.wait_ge(bias_loaded, 8 * 16)
            for cc in range(2):
                dve.tensor_scalar(neg_sink[:, :, :, 2 * cc:2 * cc + 2], sink_raw[:, :, :, :], -1.0, None, ALU.mult
                                  ).then_inc(sink_ready, 1)
            swiglu(R_FFN1, U_FFN1, S_FFN1)

            def lo_qkv(n):
                lo_of(S_QKV + n, stage_qkv[:, n % 2], w_k[:, QKV_SLOT[n % 3], 0], w_k[:, QKV_SLOT[n % 3], 1])

            def take_v(half):
                for j in range(4):
                    r = R_QKV + half * QKV_UNITS + j
                    dve.wait_ge(ring_full, r + 1)
                    dve.tensor_tensor(v_at[:, 2 * (4 * half + j) + 1, :], banks[4 + r % RING][:, 0:KV_DIM],
                                      v_bias[:, :], ALU.add).then_inc(ring_free, 1)

            def take_qk(half, j):
                r = R_QKV + half * QKV_UNITS + j + 2
                kind, i, e = QKV_TILES[j]
                dve.wait_ge(ring_full, r + 1)
                src = banks[4 + r % RING][:, :]
                if kind == "k":
                    ins = dve.tensor_scalar(k_T[:, i, half * HALF:(half + 1) * HALF], src, k_bias[:, i:i + 1], None,
                                            ALU.add)
                else:
                    ins = dve.tensor_scalar(q_T[half, i][:, :, e, :], src.rearrange("p (c q) -> p c q", q=CHUNK), q_bias[:, i, e:e + 1], DH ** -0.5,
                                            ALU.add, ALU.mult)
                ins.then_inc(ring_free, 1)

            for t in range(TT):
                add_down(R_FFN1, GROUPS - 1, t)
                if t == 0:
                    lo_qkv(0)
                    lo_qkv(1)
                norm_front(N_MIX + t)
                if t >= 2:
                    norm_back(N_MIX + t - 2)
            lo_qkv(2)
            norm_back(N_MIX + 6)
            norm_back(N_MIX + 7)
            take_v(0)
            lo_qkv(3)
            for n in range(2, 12):
                lo_qkv(n + 2)
                take_qk(0, n)
            lo_qkv(14)

            def maxima(u):
                half, i, j = u // 8, u % 8 // 4, u % 4
                for s in range(2):
                    b = 2 * u + s
                    dve.wait_ge(scores_done, b + 1)
                    step(dve.tensor_reduce(soft[:, TOP, b % 4, :], banks[s][:, :].rearrange("p (j k) -> p j k", j=4),
                                           AX.X, ALU.max, negate=True))
                    step(dve.tensor_tensor(soft[:, NEG_MAX, b % 4, :], soft[:, TOP, b % 4, :], neg_sink[:, i, s, :],
                                           ALU.min))
                    dve.tensor_tensor(soft[:, SINK_ARG, b % 4, :], soft[:, NEG_MAX, b % 4, :], neg_sink[:, i, s, :],
                                      ALU.subtract).then_inc(max_done, 1)

            def inverses(u):
                for s in range(2):
                    b = 2 * u + s
                    dve.wait_ge(exp_done, b + 1)
                    step(dve.tensor_tensor(soft[:, SUM, b % 4, :], soft[:, SUM, b % 4, :], soft[:, SINK_EXP, b % 4, :],
                                           ALU.add))
                    dve.reciprocal(soft_inv[:, b % 4, :], soft[:, SUM, b % 4, :]).then_inc(inv_done, 1)

            def take_outputs(u):
                half, i, j = u // 8, u % 8 // 4, u % 4
                t = 4 * half + j
                for s in range(2):
                    b = 2 * u + s
                    rows = slice(64 * s, 64 * s + 64)
                    dve.wait_ge(o_hi_done, b + 1)

                    def heads(v):
                        return hT[rows, v, 4 * i:4 * i + 4, t * P:(t + 1) * P].rearrange("p e (c q) -> p e c q", c=2)
                    dve.tensor_tensor(heads(1), banks[2 + s][rows, :].rearrange("p (c e q) -> p e c q", c=2, e=4),
                                      heads(0).bitcast(F32), ALU.subtract).then_inc(o_ready, 1)

            def lo_wo(m):
                slot = o_slots(m // 2)[m % 2]
                lo_of(S_O + m, stage_d[:, m % 2, :], w[:, slot, 0, :], w[:, slot, 1, :])

            def add_o(half, n):
                r = R_O + half * O_UNITS + n
                add_to_x(r, r % RING, 4 * half + n % 8 // 2, n % 2, 1.0)

            take_v(1)
            lo_qkv(15)
            tile = 2
            for u in range(8):
                maxima(u)
                if u >= 2:
                    take_outputs(u - 2)
                if u % 4 == 0:
                    take_qk(1, tile)
                    tile += 1
                inverses(u)
                for n in SPLIT_AHEAD[u]:
                    lo_qkv(n)
                take_qk(1, tile)
                tile += 1
            lo_wo(0)
            lo_wo(1)
            dve.wait_ge(b_o_added, TT)
            for u in range(8, 16):
                maxima(u)
                take_outputs(u - 2)
                n = 4 * (u - 8)
                add_o(0, n)
                add_o(0, n + 1)
                inverses(u)
                lo_wo(u - 6)
                add_o(0, n + 2)
                add_o(0, n + 3)
            take_outputs(14)
            for n in range(4):
                add_o(1, n)
            take_outputs(15)
            lo_wo(10)
            lo_wo(11)
            for n in range(4, 8):
                add_o(1, n)
            for t in range(4):
                norm_front(N_FFN2 + t)
                if t >= 1:
                    norm_back(N_FFN2 + t - 1)
                lo_wo(12 + t)
                for n in range(8 + 4 * t, 12 + 4 * t):
                    add_o(1, n)
            norm_back(N_FFN2 + 3)
            lo_gate_up(S_FFN2, 0)
            for t in range(4, TT):
                add_o(1, 24 + 2 * (t - 4))
                add_o(1, 25 + 2 * (t - 4))
                norm_front(N_FFN2 + t)
                if t == 4:
                    lo_gate_up(S_FFN2 + 2, 1)
                if t >= 6:
                    norm_back(N_FFN2 + t - 2)
            norm_back(N_FFN2 + 6)
            norm_back(N_FFN2 + 7)
            lo_down(S_FFN2 + 4)
            swiglu(R_FFN2, U_FFN2, S_FFN2)

            for t in range(TT):
                add_down(R_FFN2, GROUPS - 1, t)
                norm_front(N_FINAL + t)


_SHAPES = {
    "x": [T, D], "ffn1_norm": [D], "ffn1_w_gate": [D, F], "ffn1_w_up": [D, F], "ffn1_w_down": [F, D],
    "mix_norm": [D], "ffn2_norm": [D], "ffn2_w_gate": [D, F], "ffn2_w_up": [D, F], "ffn2_w_down": [F, D],
    "attn_w_qkv": [D, HEADS * DH + 2 * KV_DIM], "attn_b_qkv": [HEADS * DH + 2 * KV_DIM], "attn_sinks": [HEADS],
    "attn_w_o": [HEADS * DH, D], "attn_b_o": [D], "final_norm": [D],
}


def kernel(**inputs):
    import numpy as np
    import concourse.bacc as bacc
    from concourse.bass_utils import run_bass_kernel_spmd

    nc = bacc.Bacc("TRN2", target_bir_lowering=False, num_devices=1)
    arrays, args = {}, []
    for name, shape in _SHAPES.items():
        arrays[f"in_{name}"] = np.ascontiguousarray(inputs[name]).reshape(shape)
        args.append(nc.dram_tensor(f"in_{name}", shape, F32, kind="ExternalInput").ap())
    args.append(nc.dram_tensor("out_dram", [T, D], F32, kind="ExternalOutput").ap())
    trunk(nc, *args)
    result = run_bass_kernel_spmd(nc, [arrays], core_ids=[0])
    return result.results[0]["out_dram"].reshape(1, T, D)
```

```python
from contextlib import ExitStack

import concourse.bass as bass
from concourse import mybir

P = 128
T, D, F = 1024, 1024, 2816
TT, KD = T // P, D // P
HALF = 512
GROUP = 2 * P
GROUPS = F // GROUP
HEADS, KV_HEADS, DH, CHUNK = 16, 4, 64, 64
KV_DIM = KV_HEADS * DH
EPS = 1e-6
RING = 4
TURN_LAG = 3

F32, F32R = mybir.dt.float32, mybir.dt.float32r
ALU, ACT, AX = mybir.AluOpType, mybir.ActivationFunctionType, mybir.AxisListType

DOWN_UNITS = 2 * TT
QKV_UNITS = 4 + 10
O_UNITS = 32
R_FFN1 = 0
R_QKV = R_FFN1 + GROUPS * DOWN_UNITS
R_O = R_QKV + 2 * QKV_UNITS
R_FFN2 = R_O + 2 * O_UNITS
S_FFN1 = 0
S_QKV = S_FFN1 + 6 * GROUPS
S_O = S_QKV + 24
S_FFN2 = S_O + 16
U_FFN1, U_FFN2 = 0, 4 * GROUPS
N_FFN1, N_MIX, N_FFN2, N_FINAL = 0, TT, 2 * TT, 3 * TT
QKV_TILES = [("v", 0, 0), ("v", 1, 0)] + [t for i in range(2)
                                          for t in [("k", i, 0)] + [("q", i, e) for e in range(4)]]
QKV_SLOT = [1, 3, 5]
Q_SLOT = {(0, 0): 4, (0, 1): 0, (1, 0): 2, (1, 1): 4}
SPLIT_AHEAD = [[16], [17], [18], [19, 20], [21], [22], [23], []]


def o_slots(group):
    if group % 2 == 0:
        return 1, 3
    return (0, 5) if group < 4 else (4, 5)


def turn_bank(m):
    return 4 + 2 * (m % 2) if m < N_FFN1 + TT else 2


def qkv_done(n):
    half, j = divmod(n, 12)
    return R_QKV + half * QKV_UNITS + (4 if j < 2 else 4 + j - 1)


def trunk(nc, x, ffn1_norm, ffn1_w_gate, ffn1_w_up, ffn1_w_down, mix_norm, ffn2_norm,
          ffn2_w_gate, ffn2_w_up, ffn2_w_down, w_qkv, b_qkv, sinks, w_o, b_o, final_norm, out):
    ctx = ExitStack()
    base = -(-nc.sbuf_base // 64) * 64

    place = {}
    at = base
    for name, size in (("x", 32), ("hT", 64), ("w", 48), ("stage_g", 8), ("stage_u", 8),
                       ("stage_d", 8), ("act", 16), ("tmp", 8), ("hn", 16), ("norm_w", 4), ("rest", 2)):
        place[name] = at
        at += size * 1024

    def sb(name, region, shape, dt=F32, skip=0):
        return nc.alloc_sbuf_tensor_at(name, shape, dt, offset=place[region] + skip)

    x_res = sb("x_res", "x", [P, TT, D])
    hT = sb("hT", "hT", [P, 2, KD, T], F32R)
    w = sb("w", "w", [P, 6, 2, KD * P], F32R)
    w_k = w[:, :, :, :].rearrange("p s v (k c) -> p s v k c", k=KD)
    stage_g = sb("stage_g", "stage_g", [P, KD, GROUP])
    stage_u = sb("stage_u", "stage_u", [P, KD, GROUP])
    stage_d = sb("stage_d", "stage_d", [P, 2, D])
    stage_qkv = sb("stage_qkv", "stage_g", [P, 2, KD, P])
    a_T = sb("a_T", "act", [P, 2, 2, T], F32R)
    silu_g = sb("silu_g", "tmp", [P, 2, HALF])
    a_full = sb("a_full", "tmp", [P, 2, HALF], skip=4096)
    junk = sb("junk", "tmp", [P, D])
    hn = sb("hn", "hn", [P, 4, D])
    norm_w = sb("norm_w", "norm_w", [P, D])
    q_T = {key: sb(f"q_T{key[0]}{key[1]}", "w", [P, HALF // CHUNK, 4, CHUNK], skip=slot * 8192)
           for key, slot in Q_SLOT.items()}
    k_T = sb("k_T", "stage_u", [P, 2, T])
    v_at = sb("v_at", "act", [P, 2 * TT, KV_DIM])
    probs = sb("probs", "hn", [P, 4, 4, P])
    probs_T = sb("probs_T", "tmp", [P, 2, 4 * P], skip=4096)
    b_o_row = sb("b_o_row", "tmp", [P, D], skip=4096)
    ident = sb("ident", "rest", [P, P])
    v_bias = sb("v_bias", "rest", [P, KV_DIM], skip=512)
    stat = sb("stat", "rest", [P, 6, 4], skip=1536)
    SS, VAR, RVAR, R0, CORR, RSTD = range(6)
    soft = sb("soft", "rest", [P, 5, 4, 4], skip=1536 + 96)
    TOP, NEG_MAX, SINK_ARG, SINK_EXP, SUM = range(5)
    soft_inv = sb("soft_inv", "rest", [P, 4, 4], skip=1536 + 96 + 320)
    at_rest = 1536 + 96 + 320 + 64
    assert at_rest <= 2048
    place["more"] = place["rest"] + 2048
    q_bias = sb("q_bias", "more", [P, 2, 4])
    k_bias = sb("k_bias", "more", [P, 2], skip=32)
    sink_raw = sb("sink_raw", "more", [P, 2, 2, 2], skip=64)
    neg_sink = sb("neg_sink", "more", [P, 2, 2, 4], skip=96)

    with ctx:
        def sem(name):
            return ctx.enter_context(nc.semaphore(name))

        def bank(name):
            return ctx.enter_context(nc.psum_tensor(name, [P, HALF], F32))

        banks = [bank(f"bank{n}") for n in range(8)]

        x_loaded = [sem(f"x_loaded{t}") for t in range(TT)]
        norm_w_loaded = sem("norm_w_loaded")
        bias_loaded = sem("bias_loaded")
        first_loaded = sem("first_loaded")
        gate_up_loaded = sem("gate_up_loaded")
        down_loaded = sem("down_loaded")
        qkv_loaded = [sem(f"qkv_loaded{s}") for s in range(2)]
        wo_loaded = [sem(f"wo_loaded{s}") for s in range(2)]
        b_o_loaded = sem("b_o_loaded")
        stored = [sem(f"stored{s}") for s in range(4)]
        ident_ready = sem("ident_ready")
        sink_ready = sem("sink_ready")
        hi_done = sem("hi_done")
        split_done = sem("split_done")
        gate_up_done = sem("gate_up_done")
        gate_up_free = sem("gate_up_free")
        silu_done = sem("silu_done")
        a_hi_done = sem("a_hi_done")
        a_ready = sem("a_ready")
        ring_full = sem("ring_full")
        ring_free = sem("ring_free")
        square_done = sem("square_done")
        var_done = sem("var_done")
        root_done = sem("root_done")
        rstd_done = sem("rstd_done")
        weighted = sem("weighted")
        hn_done = sem("hn_done")
        turned = sem("turned")
        hT_hi_done = sem("hT_hi_done")
        hT_ready = sem("hT_ready")
        dve_step = sem("dve_step")
        b_o_added = sem("b_o_added")
        v_shifted = sem("v_shifted")
        v_zeroed = sem("v_zeroed")
        scores_done = sem("scores_done")
        max_done = sem("max_done")
        exp_done = sem("exp_done")
        probs_zeroed = sem("probs_zeroed")
        inv_done = sem("inv_done")
        probs_ready = sem("probs_ready")
        probs_turned = sem("probs_turned")
        probs_T_ready = sem("probs_T_ready")
        pv_done = sem("pv_done")
        o_hi_done = sem("o_hi_done")
        o_ready = sem("o_ready")

        wq_view = w_qkv[:, 0:HEADS * DH].rearrange("(k p) (i s e c) -> i s e p k c", p=P, i=2, s=2, e=4)
        wk_view = w_qkv[:, HEADS * DH:HEADS * DH + KV_DIM].rearrange("(k p) (i c) -> i p k c", p=P, i=2)
        wv_view = w_qkv[:, HEADS * DH + KV_DIM:].rearrange("(k p) (i c) -> i p k c", p=P, i=2)
        wo_view = w_o.rearrange("(i s e p) n -> i s e p n", i=2, s=2, e=4)

        block = ctx.enter_context(nc.Block())

        @block.sync
        def _(sp):
            def row_of(vector):
                return vector.rearrange("(o n) -> o n", o=1).broadcast_to([P, D])

            def load_norm(vector, norms_before):
                if norms_before:
                    sp.wait_ge(weighted, norms_before)
                sp.dma_start(norm_w[:, :], row_of(vector)).then_inc(norm_w_loaded, 16)

            def load_gate_up(gate, up, column):
                sp.dma_start(stage_g[:, :, :], gate[:, bass.ds(column, GROUP)].rearrange("(k p) c -> p k c", p=P)
                             ).then_inc(gate_up_loaded, 16)
                sp.dma_start(stage_u[:, :, :], up[:, bass.ds(column, GROUP)].rearrange("(k p) c -> p k c", p=P)
                             ).then_inc(gate_up_loaded, 16)

            def load_down(down, row):
                sp.dma_start(stage_d[:, :, :], down[bass.ds(row, GROUP), :].rearrange("(f p) n -> p f n", p=P)
                             ).then_inc(down_loaded, 16)

            def load_groups(gate, up, down, s0):
                with sp.Fori(0, GROUPS - 1) as i:
                    sp.wait_ge(split_done, i * 6 + (s0 + 4))
                    load_gate_up(gate, up, i * GROUP + GROUP)
                    sp.wait_ge(split_done, i * 6 + (s0 + 6))
                    load_down(down, i * GROUP + GROUP)

            def load_x(t):
                sp.dma_start(x_res[:, t, :], x[t * P:(t + 1) * P, :]).then_inc(x_loaded[t], 16)

            def load_first(f):
                for weights, stage in ((ffn1_w_gate, stage_g), (ffn1_w_up, stage_u)):
                    sp.dma_start(stage[:, :, f * P:(f + 1) * P],
                                 weights[:, f * P:(f + 1) * P].rearrange("(k p) c -> p k c", p=P)
                                 ).then_inc(first_loaded if f == 0 else gate_up_loaded, 16)

            load_x(0)
            load_norm(ffn1_norm, 0)
            for t in range(1, 4):
                load_x(t)
            load_first(0)
            for t in range(4, 6):
                load_x(t)
            load_first(1)
            for t in range(6, TT):
                load_x(t)
            load_down(ffn1_w_down, 0)
            bq = b_qkv[0:HEADS * DH].rearrange("(i s e p) -> s p i e", i=2, s=2, e=4)
            bk = b_qkv[HEADS * DH:HEADS * DH + KV_DIM].rearrange("(i p) -> p i", i=2)
            bv = b_qkv[HEADS * DH + KV_DIM:].rearrange("(o n) -> o n", o=1)
            sk = sinks.rearrange("(o i s j e) -> o e i s j", o=1, i=2, s=2, j=2)
            with nc.allow_non_contiguous_dma(reason="a few hundred words of biases and sinks"):
                for s in range(2):
                    for i in range(2):
                        sp.dma_start(q_bias[64 * s:64 * s + 64, i, :], bq[s][:, i, :]).then_inc(bias_loaded, 16)
                    sp.dma_start(sink_raw[64 * s:64 * s + 64, :, :, :],
                                 sk[:, s].broadcast_to([64, 2, 2, 2])).then_inc(bias_loaded, 16)
                sp.dma_start(k_bias[:, :], bk).then_inc(bias_loaded, 16)
            sp.dma_start(v_bias[:, :], bv.broadcast_to([P, KV_DIM])).then_inc(bias_loaded, 16)

            load_groups(ffn1_w_gate, ffn1_w_up, ffn1_w_down, S_FFN1)

            load_norm(mix_norm, N_MIX)

            def load_qkv(n):
                sp.wait_ge(split_done, S_QKV - 2 if n < 2 else S_QKV + n - 1)
                kind, i, e = QKV_TILES[n % 12]
                dst = stage_qkv[:, n % 2]
                if kind == "q":
                    for s in range(2):
                        sp.dma_start(dst[:, :, 64 * s:64 * s + 64], wq_view[i, s, e]).then_inc(qkv_loaded[n % 2], 16)
                else:
                    sp.dma_start(dst, (wk_view if kind == "k" else wv_view)[i]).then_inc(qkv_loaded[n % 2], 16)

            def load_wo(m):
                sp.wait_ge(split_done, S_QKV if m < 2 else S_O + m - 1)
                i, e = divmod(m % 8, 4)
                for s in range(2):
                    sp.dma_start(stage_d[64 * s:64 * s + 64, m % 2, :], wo_view[i, s, e]).then_inc(wo_loaded[m % 2], 16)

            for n in range(2):
                load_qkv(n)
            for m in range(2):
                load_wo(m)
            sp.wait_ge(a_ready, U_FFN2)
            sp.dma_start(b_o_row[:, :], row_of(b_o)).then_inc(b_o_loaded, 16)
            for n in range(2, 24):
                load_qkv(n)
            load_norm(ffn2_norm, N_FFN2)
            for m in range(2, 16):
                load_wo(m)
            sp.wait_ge(scores_done, 32)
            load_gate_up(ffn2_w_gate, ffn2_w_up, 0)
            sp.wait_ge(split_done, S_FFN2)
            load_down(ffn2_w_down, 0)
            load_groups(ffn2_w_gate, ffn2_w_up, ffn2_w_down, S_FFN2)
            load_norm(final_norm, N_FINAL)
            for t in range(TT):
                sp.wait_ge(hn_done, N_FINAL + t + 1)
                sp.dma_start(out[t * P:(t + 1) * P, :], hn[:, t % 4, :]).then_inc(stored[t % 4], 16)
            for s in range(4):
                sp.wait_ge(stored[s], 16 * TT // 4)

        @block.gpsimd
        def _(pool):
            pool.memset(ident[:, :], 0.0).then_inc(ident_ready, 1)
            pool.wait_ge(ident_ready, 1)
            pool.affine_select(out=ident[:, :], in_=ident[:, :], compare_op=ALU.not_equal, fill=1.0,
                               base=0, pattern=[[-1, P]], channel_multiplier=1).then_inc(ident_ready, 1)

            def weigh(m):
                t = m % TT
                pool.wait_ge(norm_w_loaded, 16 * (m // TT + 1))
                if 4 <= m < N_FINAL + 4:
                    pool.wait_ge(turned, m - 3)
                pool.tensor_tensor(hn[:, m % 4, :], x_res[:, t, :], norm_w[:, :], ALU.mult).then_inc(weighted, 1)

            for t in range(TT):
                pool.wait_ge(x_loaded[t], 16)
                weigh(N_FFN1 + t)
            for t in range(TT):
                pool.wait_ge(ring_free, RING + R_QKV - 2 * (TT - 1 - t))
                weigh(N_MIX + t)
            pool.wait_ge(b_o_loaded, 16)
            for t in range(TT):
                pool.wait_ge(square_done, N_MIX + t + 1)
                pool.tensor_tensor(x_res[:, t, :], x_res[:, t, :], b_o_row[:, :], ALU.add).then_inc(b_o_added, 1)
            pool.wait_ge(ring_full, R_QKV)
            pool.memset(v_at[0:64, 0, :], 0.0).then_inc(v_zeroed, 1)
            for b in range(32):
                pool.wait_ge(inv_done, b + 1)
                if b in (0, 1, 8, 9):
                    pool.memset(probs[:, b % 4, 0:2, 0:CHUNK], 0.0).then_inc(probs_zeroed, 1)
                    pool.wait_ge(probs_zeroed, b + 1 if b < 8 else b - 5)
                pool.tensor_tensor(probs[:, b % 4], probs[:, b % 4],
                                   soft_inv[:, b % 4, :].rearrange("p (j o) -> p j o", o=1).broadcast_to([P, 4, P]),
                                   ALU.mult).then_inc(probs_ready, 1)
            pool.wait_ge(probs_turned, 32)
            for t in range(4):
                pool.wait_ge(ring_free, RING + R_O + O_UNITS)
                weigh(N_FFN2 + t)
            for t in range(4, TT):
                pool.wait_ge(ring_free, RING + R_FFN2 - 2 * (TT - 1 - t))
                weigh(N_FFN2 + t)
            for t in range(TT - 2):
                pool.wait_ge(ring_free, RING + R_FFN2 + GROUPS * DOWN_UNITS - 2 * (TT - 1 - t))
                if t >= 4:
                    pool.wait_ge(stored[t % 4], 16)
                weigh(N_FINAL + t)

        @block.tensor
        def _(pe):
            def three_passes(psum, parts, first, last):
                mm = None
                for n, ((w_hi, w_lo), (m_hi, m_lo)) in enumerate(parts):
                    for v, (lhs, rhs) in enumerate(((w_hi, m_hi), (w_hi, m_lo), (w_lo, m_hi))):
                        mm = pe.matmul(psum, lhs, rhs, start=(first and n == 0 and v == 0),
                                       stop=(last and n == len(parts) - 1 and v == 2))
                return mm

            def columns(slot, half, ks):
                return [((w_k[:, slot, 0, k, :], w_k[:, slot, 1, k, :]),
                         (hT[:, 0, k, half * HALF:(half + 1) * HALF], hT[:, 1, k, half * HALF:(half + 1) * HALF]))
                        for k in ks]

            def gate_up(f, half):
                three_passes(banks[2 * half][:, :], columns(f, half, range(KD)), True, True)
                return three_passes(banks[2 * half + 1][:, :], columns(2 + f, half, range(KD)), True, True)

            def turn(m):
                if m in (N_FFN1, N_MIX):
                    pe.wait_ge(ident_ready, 2) if m == N_FFN1 else pe.wait_ge(gate_up_free, 2 + U_FFN2)
                if m == N_FFN2:
                    pe.wait_ge(o_ready, 32)
                if m > N_FFN1 + TT:
                    pe.wait_ge(hT_ready, m)
                elif m >= 2:
                    pe.wait_ge(hT_ready, m - 1)
                pe.wait_ge(hn_done, m + 1)
                for k in range(KD):
                    mm = pe.transpose(banks[turn_bank(m) + k // 4][:, (k % 4) * P:(k % 4 + 1) * P],
                                      hn[:, m % 4, k * P:(k + 1) * P], ident[:, :])
                mm.then_inc(turned, 1)

            def first_gate_up(u0, s0, m0, turns):
                pe.wait_ge(hT_ready, m0 + 4)
                pe.wait_ge(gate_up_free, u0 + 1)
                for n in range(KD):
                    side, k = divmod(2 * n, KD)
                    if n in turns:
                        turn(m0 + turns[n])
                    if k == 0:
                        pe.wait_ge(split_done, s0 + 1 + side)
                    mm = three_passes(banks[side][:, :], columns(2 * side, 0, (k, k + 1)), k == 0, k + 2 == KD)
                mm.then_inc(gate_up_done, 1)

            def gate_up_unit(u0, s0, i, f, half, next_group=0):
                n = i * 4 + (u0 + 4 * next_group + 2 * f + half)
                pe.wait_ge(split_done, i * 6 + (s0 + 6 * next_group + 2 * f + 2))
                pe.wait_ge(gate_up_free, n + 1)
                gate_up(f, half).then_inc(gate_up_done, 1)

            def down_unit(r0, u0, s0, i, t, dh):
                d = 2 * t + dh
                if d == 0:
                    pe.wait_ge(split_done, i * 6 + (s0 + 6))
                if dh == 0 and t % 4 == 0:
                    pe.wait_ge(a_ready, i * 4 + (u0 + 3 + t // 4))
                pe.wait_ge(ring_free, i * DOWN_UNITS + (r0 + d + 1))
                three_passes(banks[4 + (r0 + d) % RING][:, :],
                             [((a_T[:, 0, f, t * P:(t + 1) * P], a_T[:, 1, f, t * P:(t + 1) * P]),
                               (w[:, 4 + f, 0, dh * HALF:(dh + 1) * HALF], w[:, 4 + f, 1, dh * HALF:(dh + 1) * HALF]))
                              for f in range(2)], True, True).then_inc(ring_full, 1)

            def swiglu(r0, u0, s0, m_next):
                with pe.Fori(0, GROUPS - 1) as i:
                    gate_up_unit(u0, s0, i, 0, 1)
                    gate_up_unit(u0, s0, i, 1, 0)
                    gate_up_unit(u0, s0, i, 1, 1)
                    for t in range(TT):
                        for dh in range(2):
                            down_unit(r0, u0, s0, i, t, dh)
                    gate_up_unit(u0, s0, i, 0, 0, next_group=1)
                i = GROUPS - 1
                gate_up_unit(u0, s0, i, 0, 1)
                gate_up_unit(u0, s0, i, 1, 0)
                gate_up_unit(u0, s0, i, 1, 1)
                for t in range(TT):
                    for dh in range(2):
                        down_unit(r0, u0, s0, i, t, dh)
                    if m_next is not None and t >= TURN_LAG:
                        turn(m_next + t - TURN_LAG)

            for t in range(4):
                turn(N_FFN1 + t)
            first_gate_up(U_FFN1, S_FFN1, N_FFN1, {1: 4, 3: 5, 5: 6, 6: 7})
            pe.wait_ge(hT_ready, N_FFN1 + TT)
            swiglu(R_FFN1, U_FFN1, S_FFN1, N_MIX)

            def v_unit(half, j):
                r = R_QKV + half * QKV_UNITS + j
                if j == 0:
                    pe.wait_ge(hT_ready, N_MIX + 4 * half + 4)
                    pe.wait_ge(split_done, S_QKV + 12 * half + 2)
                pe.wait_ge(ring_free, r + 1)
                t = 4 * half + j
                slots = slice(QKV_SLOT[0], QKV_SLOT[1] + 1, QKV_SLOT[1] - QKV_SLOT[0])
                three_passes(banks[4 + r % RING][:, 0:KV_DIM],
                             [((hT[:, 0, k, t * P:(t + 1) * P], hT[:, 1, k, t * P:(t + 1) * P]),
                               (w_k[:, slots, 0, k, :], w_k[:, slots, 1, k, :]))
                              for k in range(KD)], True, True).then_inc(ring_full, 1)

            def qk_unit(half, j, part=None):
                r = R_QKV + half * QKV_UNITS + j + 2
                if part != 1:
                    pe.wait_ge(split_done, S_QKV + 12 * half + j + 1)
                    pe.wait_ge(ring_free, r + 1)
                ks = range(KD) if part is None else range(4 * part, 4 * part + 4)
                mm = three_passes(banks[4 + r % RING][:, :], columns(QKV_SLOT[j % 3], half, ks),
                                  part != 1, part != 0)
                if part != 0:
                    mm.then_inc(ring_full, 1)

            def o_unit(half, n):
                g, rest = divmod(n, 8)
                j, dh = divmod(rest, 2)
                t = 4 * half + j
                r = R_O + half * O_UNITS + n
                if rest == 0:
                    pe.wait_ge(split_done, S_O + 2 * (4 * half + g) + 2)
                pe.wait_ge(o_ready, 16 * half + 8 * (g // 2) + 2 * j + 2)
                pe.wait_ge(ring_free, r + 1)
                three_passes(banks[4 + r % RING][:, :],
                             [((hT[:, 0, 2 * g + f, t * P:(t + 1) * P], hT[:, 1, 2 * g + f, t * P:(t + 1) * P]),
                               (w[:, o_slots(4 * half + g)[f], 0, dh * HALF:(dh + 1) * HALF],
                                w[:, o_slots(4 * half + g)[f], 1, dh * HALF:(dh + 1) * HALF]))
                              for f in range(2)], True, True).then_inc(ring_full, 1)

            def scores(u):
                half, i, j = u // 8, u % 8 // 4, u % 4
                pe.wait_ge(ring_free, RING + R_QKV + half * QKV_UNITS + (9 if i == 0 else 14))
                if u >= 1:
                    pe.wait_ge(exp_done, 2 * u)
                for s in range(2):
                    rows = slice(64 * s, 64 * s + 64)
                    for cc in range(2):
                        c = 2 * (4 * half + j) + cc
                        for pair in range(2):
                            lhs = q_T[half, i][rows, 2 * j + cc, 2 * pair:2 * pair + 2, :].rearrange("p e q -> p (e q)")
                            col = (2 * cc + pair) * P
                            if c == 0:
                                for n in range(2):
                                    mm = pe.matmul(banks[s][:, col + 64 * n:col + 64 * n + 64], lhs,
                                                   k_T[rows, i, 0:64], start=True, stop=True)
                            else:
                                mm = pe.matmul(banks[s][:, col:col + P], lhs,
                                               k_T[rows, i, 64 * (c - 1):64 * (c + 1)], start=True, stop=True)
                    mm.then_inc(scores_done, 1)

            def turn_probs(u):
                for s in range(2):
                    b = 2 * u + s
                    pe.wait_ge(probs_ready, b + 1)
                    if b >= 2:
                        pe.wait_ge(o_ready, b - 1)
                    else:
                        pe.wait_ge(hT_ready, N_MIX + TT)
                    for block_ in range(4):
                        mm = pe.transpose(banks[2 + s][:, block_ * P:(block_ + 1) * P], probs[:, b % 4, block_, :], ident[:, :])
                    mm.then_inc(probs_turned, 1)

            def times_v(u):
                half, i, j = u // 8, u % 8 // 4, u % 4
                for s in range(2):
                    b = 2 * u + s
                    pe.wait_ge(probs_T_ready, b + 1)
                    if s == 0:
                        pe.wait_ge(v_shifted, 2 * (4 * half + j) + 1)
                        if u == 0:
                            pe.wait_ge(v_zeroed, 1)
                    for cc in range(2):
                        c = 2 * (4 * half + j) + cc
                        mm = pe.matmul(banks[2 + s][:, cc * 256:(cc + 1) * 256], v_at[:, c, i * P:(i + 1) * P],
                                       probs_T[:, s, cc * 256:(cc + 1) * 256], start=True, stop=True)
                    mm.then_inc(pv_done, 1)

            for j in range(4):
                v_unit(0, j)
                if j < TURN_LAG:
                    turn(N_MIX + TT - TURN_LAG + j)
            for j in range(2, 12):
                qk_unit(0, j)
            pe.wait_ge(hT_ready, N_MIX + TT)
            for j in range(4):
                v_unit(1, j)
            tile = 2
            for u in range(8):
                scores(u)
                if u % 4 == 0:
                    qk_unit(1, tile)
                    tile += 1
                qk_unit(1, tile, part=0)
                if u >= 1:
                    turn_probs(u - 1)
                qk_unit(1, tile, part=1)
                tile += 1
                if u >= 1:
                    times_v(u - 1)
            for u in range(8, 16):
                scores(u)
                o_unit(0, 4 * (u - 8))
                o_unit(0, 4 * (u - 8) + 1)
                turn_probs(u - 1)
                o_unit(0, 4 * (u - 8) + 2)
                o_unit(0, 4 * (u - 8) + 3)
                times_v(u - 1)
            for n in range(4):
                o_unit(1, n)
            turn_probs(15)
            for n in range(4, 8):
                o_unit(1, n)
            times_v(15)
            for n in range(8, 32):
                o_unit(1, n)
                if n in (15, 18, 21, 24):
                    turn(N_FFN2 + (n - 15) // 3)
                if n == 30:
                    turn(N_FFN2 + 4)

            first_gate_up(U_FFN2, S_FFN2, N_FFN2, {2: 5, 4: 6, 6: 7})
            pe.wait_ge(hT_ready, N_FFN2 + TT)
            swiglu(R_FFN2, U_FFN2, S_FFN2, None)

        @block.scalar
        def _(act):
            def hi_of(stage, slot_view):
                act.activation(slot_view, stage, ACT.Copy).then_inc(hi_done, 1)

            def hi_gate_up(f):
                hi_of(stage_g[:, :, f * P:(f + 1) * P], w_k[:, f, 0])
                hi_of(stage_u[:, :, f * P:(f + 1) * P], w_k[:, 2 + f, 0])

            def hi_down():
                for f in range(2):
                    hi_of(stage_d[:, f, :], w[:, 4 + f, 0, :])

            def square(m):
                if m >= 4:
                    act.wait_ge(rstd_done, m - 3)
                if m >= 1:
                    act.wait_ge(square_done, m)
                act.activation(junk[:, :], x_res[:, m % TT, :], ACT.Square,
                               accum_out=stat[:, SS, m % 4:m % 4 + 1]).then_inc(square_done, 1)

            def root(m, tiles=1):
                act.wait_ge(var_done, m + tiles)
                act.activation(stat[:, R0, m % 4:m % 4 + tiles], stat[:, RVAR, m % 4:m % 4 + tiles],
                               ACT.Sqrt).then_inc(root_done, tiles)

            def scale(m):
                act.wait_ge(rstd_done, m + 1)
                act.wait_ge(weighted, m + 1)
                act.activation(hn[:, m % 4, :], hn[:, m % 4, :], ACT.Copy,
                               scale=stat[:, RSTD, m % 4:m % 4 + 1]).then_inc(hn_done, 1)

            def norm_back(m):
                t = m % TT
                act.wait_ge(turned, m + 1)
                for q in range(2):
                    act.activation(hT[:, 0, 4 * q:4 * q + 4, t * P:(t + 1) * P],
                                   banks[turn_bank(m) + q][:, :].rearrange("p (k c) -> p k c", k=4), ACT.Copy
                                   ).then_inc(hT_hi_done, 1)

            def hidden(u0, i, f, half):
                n = i * 4 + (u0 + 2 * f + half)
                act.wait_ge(gate_up_done, n + 1)
                act.wait_ge(gate_up_free, n + 1)
                act.activation(silu_g[:, half, :], banks[2 * half][:, :], ACT.Silu).then_inc(silu_done, 1)
                act.wait_ge(gate_up_free, n + 3)
                act.activation(a_T[:, 0, f, half * HALF:(half + 1) * HALF], a_full[:, half, :], ACT.Copy
                               ).then_inc(a_hi_done, 1)

            def swiglu(r0, u0, l0):
                with act.Fori(0, GROUPS - 1) as i:
                    hidden(u0, i, 0, 0)
                    hidden(u0, i, 0, 1)
                    act.wait_ge(gate_up_loaded, i * 32 + 32 * (l0 + 2))
                    hi_gate_up(0)
                    hidden(u0, i, 1, 0)
                    hidden(u0, i, 1, 1)
                    hi_gate_up(1)
                    act.wait_ge(down_loaded, i * 16 + 16 * (l0 + 2))
                    act.wait_ge(ring_full, i * DOWN_UNITS + (r0 + DOWN_UNITS))
                    hi_down()
                for f in range(2):
                    for half in range(2):
                        hidden(u0, GROUPS - 1, f, half)

            act.wait_ge(ring_free, RING)
            act.activation(stat[:, R0, 0:1], stat[:, RSTD, 0:1], ACT.Sqrt)
            for t in range(TT):
                act.wait_ge(x_loaded[t], 16)
                square(N_FFN1 + t)
                if t in (2, 3, 6, 7):
                    norm_back(N_FFN1 + t - 2)
                root(N_FFN1 + t)
                if t == 3:
                    act.wait_ge(first_loaded, 32)
                    hi_of(stage_g[:, :, 0:P], w_k[:, 0, 0])
                    norm_back(N_FFN1 + 2)
                    norm_back(N_FFN1 + 3)
                    hi_of(stage_u[:, :, 0:P], w_k[:, 2, 0])
            norm_back(N_FFN1 + TT - 2)
            act.wait_ge(gate_up_loaded, 32)
            hi_of(stage_g[:, :, P:2 * P], w_k[:, 1, 0])
            norm_back(N_FFN1 + TT - 1)
            hi_of(stage_u[:, :, P:2 * P], w_k[:, 3, 0])
            act.wait_ge(down_loaded, 16)
            hi_down()
            swiglu(R_FFN1, U_FFN1, 0)

            loads = [0, 0]

            def hi_qkv(n):
                loads[n % 2] += 32 if QKV_TILES[n % 12][0] == "q" else 16
                act.wait_ge(qkv_loaded[n % 2], loads[n % 2])
                if n < 3:
                    act.wait_ge(ring_full, R_QKV) if n == 2 else act.wait_ge(gate_up_done, U_FFN2)
                else:
                    act.wait_ge(ring_full, qkv_done(n - 3))
                hi_of(stage_qkv[:, n % 2], w_k[:, QKV_SLOT[n % 3], 0])

            for n in range(2):
                hi_qkv(n)
            for t in range(TT):
                if t >= 1:
                    root(N_MIX + t - 1)
                if t >= TURN_LAG:
                    norm_back(N_MIX + t - TURN_LAG)
                act.wait_ge(ring_free, RING + R_QKV - 2 * (TT - 1 - t))
                square(N_MIX + t)
                if t >= 1:
                    scale(N_MIX + t - 1)
            root(N_MIX + TT - 1)
            for t in range(TT - TURN_LAG, TT):
                norm_back(N_MIX + t)
                if t == TT - TURN_LAG:
                    scale(N_MIX + TT - 1)
                    hi_qkv(2)

            def shift_v(half):
                for t in range(4 * half, 4 * half + 4):
                    act.wait_ge(ring_free, RING + R_QKV + half * QKV_UNITS + t % 4 + 1)
                    act.activation(v_at[64:128, 2 * t, :], v_at[0:64, 2 * t + 1, :], ACT.Copy).then_inc(v_shifted, 1)
                    if t < TT - 1:
                        act.activation(v_at[0:64, 2 * t + 2, :], v_at[64:128, 2 * t + 1, :], ACT.Copy
                                       ).then_inc(v_shifted, 1)

            hi_qkv(3)
            shift_v(0)
            for n in range(4, 15):
                hi_qkv(n)

            def exps(u):
                half, i, j = u // 8, u % 8 // 4, u % 4
                for s in range(2):
                    b = 2 * u + s
                    act.wait_ge(max_done, b + 1)
                    if b >= 4:
                        act.wait_ge(probs_turned, b - 3)
                    else:
                        act.wait_ge(turned, N_MIX + TT)
                    first = [n for n in range(4) if u % 4 == 0 and u < 8 and n < 2]
                    for n in range(4):
                        lo = 64 if n in first else 0
                        act.activation(probs[:, b % 4, n, lo:], banks[s][:, n * P + lo:(n + 1) * P], ACT.Exp,
                                       bias=soft[:, NEG_MAX, b % 4, n:n + 1],
                                       accum_out=soft[:, SUM, b % 4, n:n + 1])
                    act.activation(soft[:, SINK_EXP, b % 4, :], soft[:, SINK_ARG, b % 4, :], ACT.Exp
                                   ).then_inc(exp_done, 1)

            def take_probs(u):
                for s in range(2):
                    b = 2 * u + s
                    act.wait_ge(probs_turned, b + 1)
                    if b >= 2:
                        act.wait_ge(pv_done, b - 1)
                    else:
                        act.wait_ge(b_o_added, TT)
                    act.activation(probs_T[:, s, :], banks[2 + s][:, :], ACT.Copy).then_inc(probs_T_ready, 1)

            def take_outputs(u):
                half, i, j = u // 8, u % 8 // 4, u % 4
                t = 4 * half + j
                for s in range(2):
                    b = 2 * u + s
                    rows = slice(64 * s, 64 * s + 64)
                    act.wait_ge(pv_done, b + 1)
                    act.activation(
                        hT[rows, 0, 4 * i:4 * i + 4, t * P:(t + 1) * P].rearrange("p e (c q) -> p e c q", c=2),
                        banks[2 + s][rows, :].rearrange("p (c e q) -> p e c q", c=2, e=4), ACT.Copy
                    ).then_inc(o_hi_done, 1)

            def hi_wo(m):
                g = m // 2
                act.wait_ge(wo_loaded[m % 2], 32 * (m // 2 + 1))
                slot = o_slots(g)[m % 2]
                if g == 0:
                    act.wait_ge(ring_full, qkv_done(21 + m))
                elif g == 1:
                    act.wait_ge(scores_done, 16) if slot == 0 else act.wait_ge(ring_full, qkv_done(23))
                elif slot == 4 and g == 5:
                    act.wait_ge(scores_done, 32)
                else:
                    act.wait_ge(ring_full, R_O + 8 * (g - 1))
                hi_of(stage_d[:, m % 2, :], w[:, slot, 0, :])

            hi_qkv(15)
            for u in range(8):
                if u >= 2:
                    take_outputs(u - 2)
                exps(u)
                if u >= 1:
                    take_probs(u - 1)
                for n in SPLIT_AHEAD[u]:
                    hi_qkv(n)
                if u == 0:
                    shift_v(1)
                if u == 7:
                    hi_wo(0)
                    hi_wo(1)
            for u in range(8, 16):
                take_outputs(u - 2)
                exps(u)
                take_probs(u - 1)
                hi_wo(u - 6)
            take_outputs(14)
            take_probs(15)
            hi_wo(10)
            hi_wo(11)
            act.wait_ge(ring_free, RING + R_O + O_UNITS)
            for t in range(4):
                square(N_FFN2 + t)
            root(N_FFN2, 4)
            take_outputs(15)
            scale(N_FFN2)
            scale(N_FFN2 + 1)
            hi_wo(12)
            hi_wo(13)
            norm_back(N_FFN2)
            scale(N_FFN2 + 2)
            norm_back(N_FFN2 + 1)
            scale(N_FFN2 + 3)
            hi_wo(14)
            hi_wo(15)
            act.wait_ge(gate_up_loaded, 32 * (GROUPS + 1))
            norm_back(N_FFN2 + 2)
            hi_gate_up(0)
            norm_back(N_FFN2 + 3)
            for t in range(4, TT):
                if t > 4:
                    root(N_FFN2 + t - 1)
                if t == 7:
                    norm_back(N_FFN2 + 4)
                act.wait_ge(ring_free, RING + R_FFN2 - 2 * (TT - 1 - t))
                square(N_FFN2 + t)
                if t > 4:
                    scale(N_FFN2 + t - 1)
            root(N_FFN2 + TT - 1)
            norm_back(N_FFN2 + 5)
            scale(N_FFN2 + TT - 1)
            norm_back(N_FFN2 + 6)
            norm_back(N_FFN2 + 7)
            act.wait_ge(ring_full, R_O + 8 * 7)
            hi_gate_up(1)
            act.wait_ge(down_loaded, 16 * (GROUPS + 1))
            act.wait_ge(ring_full, R_FFN2)
            hi_down()
            swiglu(R_FFN2, U_FFN2, GROUPS)

            for t in range(TT):
                if t >= 1:
                    root(N_FINAL + t - 1)
                act.wait_ge(ring_free, RING + R_FFN2 + GROUPS * DOWN_UNITS - 2 * (TT - 1 - t))
                square(N_FINAL + t)
                if 1 <= t < TT - 1:
                    scale(N_FINAL + t - 1)
            root(N_FINAL + TT - 1)

        @block.vector
        def _(dve):
            steps = [0]

            def step(ins):
                steps[0] += 1
                ins.then_inc(dve_step, 1)
                dve.wait_ge(dve_step, steps[0])

            def lo_of(n, stage, hi, lo):
                dve.wait_ge(hi_done, n + 1)
                dve.tensor_tensor(lo, stage, hi.bitcast(F32), ALU.subtract).then_inc(split_done, 1)

            def lo_gate_up(n, f):
                lo_of(n, stage_g[:, :, f * P:(f + 1) * P], w_k[:, f, 0], w_k[:, f, 1])
                lo_of(n + 1, stage_u[:, :, f * P:(f + 1) * P], w_k[:, 2 + f, 0], w_k[:, 2 + f, 1])

            def lo_down(n):
                for f in range(2):
                    lo_of(n + f, stage_d[:, f, :], w[:, 4 + f, 0, :], w[:, 4 + f, 1, :])

            def variance(m, tiles=1):
                c = slice(m % 4, m % 4 + tiles)
                dve.wait_ge(square_done, m + tiles)
                step(dve.tensor_scalar(stat[:, VAR, c], stat[:, SS, c], 1.0 / D, EPS, ALU.mult, ALU.add))
                dve.reciprocal(stat[:, RVAR, c], stat[:, VAR, c]).then_inc(var_done, tiles)

            def rstd(m, tiles=1):
                c = slice(m % 4, m % 4 + tiles)
                dve.wait_ge(root_done, m + tiles)
                if tiles == 1:
                    step(dve.scalar_tensor_tensor(out=stat[:, CORR, c], in0=stat[:, R0, c], scalar=stat[:, R0, c],
                                                  in1=stat[:, VAR, c], op0=ALU.mult, op1=ALU.mult))
                else:
                    step(dve.tensor_tensor(stat[:, CORR, c], stat[:, R0, c], stat[:, R0, c], ALU.mult))
                    step(dve.tensor_tensor(stat[:, CORR, c], stat[:, CORR, c], stat[:, VAR, c], ALU.mult))
                step(dve.tensor_scalar(stat[:, CORR, c], stat[:, CORR, c], -0.5, 1.5, ALU.mult, ALU.add))
                dve.tensor_tensor(stat[:, RSTD, c], stat[:, R0, c], stat[:, CORR, c], ALU.mult).then_inc(rstd_done, tiles)

            def scale(m):
                dve.wait_ge(rstd_done, m + 1)
                dve.wait_ge(weighted, m + 1)
                dve.tensor_scalar(hn[:, m % 4, :], hn[:, m % 4, :], stat[:, RSTD, m % 4:m % 4 + 1], None,
                                  ALU.mult).then_inc(hn_done, 1)

            def finish(m):
                t = m % TT
                dve.wait_ge(rstd_done, m + 1)
                dve.wait_ge(norm_w_loaded, 16 * (m // TT + 1))
                if t >= 4:
                    dve.wait_ge(stored[m % 4], 16 * (t // 4))
                dve.scalar_tensor_tensor(out=hn[:, m % 4, :], in0=x_res[:, t, :], scalar=stat[:, RSTD, m % 4:m % 4 + 1],
                                         in1=norm_w[:, :], op0=ALU.mult, op1=ALU.mult).then_inc(hn_done, 1)

            def norm_back(m):
                t = m % TT
                for q in range(2):
                    dve.wait_ge(hT_hi_done, 2 * m + q + 1)
                    ins = dve.tensor_tensor(hT[:, 1, 4 * q:4 * q + 4, t * P:(t + 1) * P],
                                            banks[turn_bank(m) + q][:, :].rearrange("p (k c) -> p k c", k=4),
                                            hT[:, 0, 4 * q:4 * q + 4, t * P:(t + 1) * P].bitcast(F32), ALU.subtract)
                ins.then_inc(hT_ready, 1)

            def hidden(u0, i, f, half):
                n = i * 4 + (u0 + 2 * f + half)
                dve.wait_ge(silu_done, n + 1)
                dve.tensor_tensor(a_full[:, half, :], silu_g[:, half, :], banks[2 * half + 1][:, :], ALU.mult
                                  ).then_inc(gate_up_free, 1)
                dve.wait_ge(a_hi_done, n + 1)
                cols = slice(half * HALF, (half + 1) * HALF)
                dve.tensor_tensor(a_T[:, 1, f, cols], a_full[:, half, :], a_T[:, 0, f, cols].bitcast(F32),
                                  ALU.subtract).then_inc(a_ready, 1)

            def add_to_x(r, bank_, t, dh, factor):
                dve.wait_ge(ring_full, r + 1)
                cols = x_res[:, t, dh * HALF:(dh + 1) * HALF]
                dve.scalar_tensor_tensor(out=cols, in0=banks[4 + bank_][:, :], scalar=factor, in1=cols,
                                         op0=ALU.mult, op1=ALU.add).then_inc(ring_free, 1)

            def add_down(r0, i, t):
                for dh in range(2):
                    add_to_x(i * DOWN_UNITS + (r0 + 2 * t + dh), (r0 + 2 * t + dh) % RING, t, dh, 0.5)

            def swiglu(r0, u0, s0):
                with dve.Fori(0, GROUPS - 1) as i:
                    hidden(u0, i, 0, 0)
                    hidden(u0, i, 0, 1)
                    lo_gate_up(i * 6 + (s0 + 6), 0)
                    hidden(u0, i, 1, 0)
                    hidden(u0, i, 1, 1)
                    add_down(r0, i, 0)
                    add_down(r0, i, 1)
                    lo_gate_up(i * 6 + (s0 + 8), 1)
                    for t in range(2, TT):
                        add_down(r0, i, t)
                    lo_down(i * 6 + (s0 + 10))
                for f in range(2):
                    for half in range(2):
                        hidden(u0, GROUPS - 1, f, half)

            dve.memset(stat[:, RSTD, 0:1], 1.0).then_inc(ring_free, RING)
            dve.memset(stat[:, RSTD, 1:2], 1.0).then_inc(gate_up_free, 2)

            for t in range(TT):
                variance(N_FFN1 + t)
                if t in (2, 3, 6, 7):
                    norm_back(N_FFN1 + t - 2)
                rstd(N_FFN1 + t)
                scale(N_FFN1 + t)
                if t == 3:
                    lo_of(S_FFN1, stage_g[:, :, 0:P], w_k[:, 0, 0], w_k[:, 0, 1])
                    norm_back(N_FFN1 + 2)
                    norm_back(N_FFN1 + 3)
                    lo_of(S_FFN1 + 1, stage_u[:, :, 0:P], w_k[:, 2, 0], w_k[:, 2, 1])
            norm_back(N_FFN1 + TT - 2)
            lo_of(S_FFN1 + 2, stage_g[:, :, P:2 * P], w_k[:, 1, 0], w_k[:, 1, 1])
            norm_back(N_FFN1 + TT - 1)
            lo_of(S_FFN1 + 3, stage_u[:, :, P:2 * P], w_k[:, 3, 0], w_k[:, 3, 1])
            lo_down(S_FFN1 + 4)
            dve.wait_ge(bias_loaded, 8 * 16)
            for cc in range(2):
                dve.tensor_scalar(neg_sink[:, :, :, 2 * cc:2 * cc + 2], sink_raw[:, :, :, :], -1.0, None, ALU.mult
                                  ).then_inc(sink_ready, 1)
            swiglu(R_FFN1, U_FFN1, S_FFN1)

            def lo_qkv(n):
                lo_of(S_QKV + n, stage_qkv[:, n % 2], w_k[:, QKV_SLOT[n % 3], 0], w_k[:, QKV_SLOT[n % 3], 1])

            def take_v(half, j):
                r = R_QKV + half * QKV_UNITS + j
                dve.wait_ge(ring_full, r + 1)
                dve.tensor_tensor(v_at[:, 2 * (4 * half + j) + 1, :], banks[4 + r % RING][:, 0:KV_DIM],
                                  v_bias[:, :], ALU.add).then_inc(ring_free, 1)

            def take_qk(half, j):
                r = R_QKV + half * QKV_UNITS + j + 2
                kind, i, e = QKV_TILES[j]
                dve.wait_ge(ring_full, r + 1)
                src = banks[4 + r % RING][:, :]
                if kind == "k":
                    ins = dve.tensor_scalar(k_T[:, i, half * HALF:(half + 1) * HALF], src, k_bias[:, i:i + 1], None,
                                            ALU.add)
                else:
                    ins = dve.tensor_scalar(q_T[half, i][:, :, e, :], src.rearrange("p (c q) -> p c q", q=CHUNK), q_bias[:, i, e:e + 1], DH ** -0.5,
                                            ALU.add, ALU.mult)
                ins.then_inc(ring_free, 1)

            for t in range(TT):
                if t >= 1:
                    variance(N_MIX + t - 1)
                add_down(R_FFN1, GROUPS - 1, t)
                if t == 0:
                    lo_qkv(0)
                    lo_qkv(1)
                if t >= TURN_LAG:
                    norm_back(N_MIX + t - TURN_LAG)
                if t >= 1:
                    rstd(N_MIX + t - 1)
            variance(N_MIX + TT - 1)
            rstd(N_MIX + TT - 1)
            for j in range(4):
                take_v(0, j)
                if j < TURN_LAG:
                    norm_back(N_MIX + TT - TURN_LAG + j)
                if j == 0:
                    lo_qkv(2)
            lo_qkv(3)
            for n in range(2, 12):
                lo_qkv(n + 2)
                take_qk(0, n)
            lo_qkv(14)

            def maxima(u):
                half, i, j = u // 8, u % 8 // 4, u % 4
                for s in range(2):
                    b = 2 * u + s
                    dve.wait_ge(scores_done, b + 1)
                    step(dve.tensor_reduce(soft[:, TOP, b % 4, :], banks[s][:, :].rearrange("p (j k) -> p j k", j=4),
                                           AX.X, ALU.max, negate=True))
                    step(dve.tensor_tensor(soft[:, NEG_MAX, b % 4, :], soft[:, TOP, b % 4, :], neg_sink[:, i, s, :],
                                           ALU.min))
                    dve.tensor_tensor(soft[:, SINK_ARG, b % 4, :], soft[:, NEG_MAX, b % 4, :], neg_sink[:, i, s, :],
                                      ALU.subtract).then_inc(max_done, 1)

            def inverses(u):
                for s in range(2):
                    b = 2 * u + s
                    dve.wait_ge(exp_done, b + 1)
                    step(dve.tensor_tensor(soft[:, SUM, b % 4, :], soft[:, SUM, b % 4, :], soft[:, SINK_EXP, b % 4, :],
                                           ALU.add))
                    dve.reciprocal(soft_inv[:, b % 4, :], soft[:, SUM, b % 4, :]).then_inc(inv_done, 1)

            def take_outputs(u):
                half, i, j = u // 8, u % 8 // 4, u % 4
                t = 4 * half + j
                for s in range(2):
                    b = 2 * u + s
                    rows = slice(64 * s, 64 * s + 64)
                    dve.wait_ge(o_hi_done, b + 1)

                    def heads(v):
                        return hT[rows, v, 4 * i:4 * i + 4, t * P:(t + 1) * P].rearrange("p e (c q) -> p e c q", c=2)
                    dve.tensor_tensor(heads(1), banks[2 + s][rows, :].rearrange("p (c e q) -> p e c q", c=2, e=4),
                                      heads(0).bitcast(F32), ALU.subtract).then_inc(o_ready, 1)

            def lo_wo(m):
                slot = o_slots(m // 2)[m % 2]
                lo_of(S_O + m, stage_d[:, m % 2, :], w[:, slot, 0, :], w[:, slot, 1, :])

            def add_o(half, n):
                r = R_O + half * O_UNITS + n
                add_to_x(r, r % RING, 4 * half + n % 8 // 2, n % 2, 1.0)

            for j in range(4):
                take_v(1, j)
            lo_qkv(15)
            tile = 2
            for u in range(8):
                maxima(u)
                if u >= 2:
                    take_outputs(u - 2)
                if u % 4 == 0:
                    take_qk(1, tile)
                    tile += 1
                inverses(u)
                for n in SPLIT_AHEAD[u]:
                    lo_qkv(n)
                take_qk(1, tile)
                tile += 1
                if u == 7:
                    lo_wo(0)
                    lo_wo(1)
            dve.wait_ge(b_o_added, TT)
            for u in range(8, 16):
                maxima(u)
                take_outputs(u - 2)
                n = 4 * (u - 8)
                add_o(0, n)
                add_o(0, n + 1)
                inverses(u)
                lo_wo(u - 6)
                add_o(0, n + 2)
                add_o(0, n + 3)
            take_outputs(14)
            for n in range(4):
                add_o(1, n)
            lo_wo(10)
            lo_wo(11)
            for n in range(4, 8):
                add_o(1, n)
            variance(N_FFN2, 4)
            add_o(1, 8)
            take_outputs(15)
            rstd(N_FFN2, 4)
            for n in range(9, 24):
                add_o(1, n)
                if n in (12, 13):
                    lo_wo(n)
                if n in (16, 19):
                    norm_back(N_FFN2 + (n - 16) // 3)
                if n in (20, 21):
                    lo_wo(n - 6)
                if n == 22:
                    norm_back(N_FFN2 + 2)
                if n == 23:
                    lo_gate_up(S_FFN2, 0)
            for t in range(4, TT):
                if t > 4:
                    variance(N_FFN2 + t - 1)
                add_o(1, 16 + 2 * t)
                add_o(1, 17 + 2 * t)
                if t in (4, 7):
                    norm_back(N_FFN2 + (3 if t == 4 else 4))
                if t > 4:
                    rstd(N_FFN2 + t - 1)
            variance(N_FFN2 + TT - 1)
            rstd(N_FFN2 + TT - 1)
            for t in range(5, TT):
                norm_back(N_FFN2 + t)
            lo_gate_up(S_FFN2 + 2, 1)
            lo_down(S_FFN2 + 4)
            swiglu(R_FFN2, U_FFN2, S_FFN2)

            for t in range(TT):
                if t >= 1:
                    variance(N_FINAL + t - 1)
                add_down(R_FFN2, GROUPS - 1, t)
                if t >= 1:
                    rstd(N_FINAL + t - 1)
                if t == TT - 1:
                    finish(N_FINAL + t - 1)
            variance(N_FINAL + TT - 1)
            rstd(N_FINAL + TT - 1)
            finish(N_FINAL + TT - 1)


_SHAPES = {
    "x": [T, D], "ffn1_norm": [D], "ffn1_w_gate": [D, F], "ffn1_w_up": [D, F], "ffn1_w_down": [F, D],
    "mix_norm": [D], "ffn2_norm": [D], "ffn2_w_gate": [D, F], "ffn2_w_up": [D, F], "ffn2_w_down": [F, D],
    "attn_w_qkv": [D, HEADS * DH + 2 * KV_DIM], "attn_b_qkv": [HEADS * DH + 2 * KV_DIM], "attn_sinks": [HEADS],
    "attn_w_o": [HEADS * DH, D], "attn_b_o": [D], "final_norm": [D],
}


def kernel(**inputs):
    import numpy as np
    import concourse.bacc as bacc
    from concourse.bass_utils import run_bass_kernel_spmd

    nc = bacc.Bacc("TRN2", target_bir_lowering=False, num_devices=1,
                   dynamic_dma_scratch_size=8192)
    arrays, args = {}, []
    for name, shape in _SHAPES.items():
        arrays[f"in_{name}"] = np.ascontiguousarray(inputs[name]).reshape(shape)
        args.append(nc.dram_tensor(f"in_{name}", shape, F32, kind="ExternalInput").ap())
    args.append(nc.dram_tensor("out_dram", [T, D], F32, kind="ExternalOutput").ap())
    trunk(nc, *args)
    result = run_bass_kernel_spmd(nc, [arrays], core_ids=[0])
    return result.results[0]["out_dram"].reshape(1, T, D)
```
